# Optimizing a Trainium2 kernel written in Bass

```python
import jax, jax.numpy as jnp
from jax import lax
import numpy as np

D_MODEL = 1024
BATCH = 1
SEQ = 256
DEPTH = 2

RWKV_HEADS = 6
RWKV_HEAD_DIM = 64
RWKV_WIDTH = RWKV_HEADS * RWKV_HEAD_DIM
W_LORA = 64
A_LORA = 64
G_LORA = 128
RET_HEADS = 6
RET_HEAD_DIM = 64
RET_WIDTH = RET_HEADS * RET_HEAD_DIM
RET_CHUNK = 128
POOL_GROUPS = 4
POOL_GROUP_DIM = 64
POOL_WIDTH = POOL_GROUPS * POOL_GROUP_DIM
POOL_WINDOWS = (2, 4, 8, 16)
MIX_WIDTH = RWKV_WIDTH + RET_WIDTH + POOL_WIDTH
RWKV_COLS = 3 * RWKV_WIDTH + W_LORA + A_LORA + G_LORA
RET_COLS = 4 * RET_WIDTH
IN_COLS = RWKV_COLS + RET_COLS + POOL_WIDTH
N_EXPERTS = 64
TOP_K = 8
N_GROUPS = 8
TOPK_GROUPS = 4
EXPERT_HIDDEN = 256
SHARED_HIDDEN = 256
ROUTED_SCALE = 2.5
MOE_BLOCK = 256
NORM_EPS = 1e-6
RWKV_LNX_EPS = 64e-5
RET_NORM_EPS = 1e-6
ROPE_BASE = 10000.0

kernel_name = 'hybrid_rwkv7_retention_pool_moe_adaln'

def rms_norm(x, g):
    xf = x.astype(jnp.float32)
    y = xf * lax.rsqrt(jnp.mean(xf * xf, -1, keepdims=True) + NORM_EPS)
    return (y * g.astype(jnp.float32)).astype(x.dtype)

def token_shift(p, mu):
    prev = jnp.pad(p, ((0, 0), (1, 0), (0, 0)))[:, :-1]
    return p + (prev - p) * mu

def group_norm(y, w, b, eps):
    B, T, H, d = y.shape
    mu = jnp.mean(y, -1, keepdims=True)
    var = jnp.mean(jnp.square(y - mu), -1, keepdims=True)
    yn = (y - mu) * lax.rsqrt(var + eps)
    return yn.reshape(B, T, H * d) * w + b

def rwkv7_scan(r, decay, k, v, kk, a):
    def step(S, inp):
        r_t, w_t, k_t, v_t, kk_t, a_t = inp
        sa = jnp.einsum('bhij,bhj->bhi', S, -kk_t)
        S = (S * w_t[:, :, None, :] + sa[..., None] * (kk_t * a_t)[:, :, None, :]
             + v_t[..., None] * k_t[:, :, None, :])
        return S, jnp.einsum('bhij,bhj->bhi', S, r_t)
    B, T, H, d = r.shape
    xs = tuple(jnp.moveaxis(t, 1, 0) for t in (r, decay, k, v, kk, a))
    _, ys = lax.scan(step, jnp.zeros((B, H, d, d), jnp.float32), xs)
    return jnp.moveaxis(ys, 0, 1)

def rwkv7_mixer(p, mu, w_up, w0, a_up, a0, g_up, k_k, k_a, r_k, lnx_w, lnx_b):
    B, T, _ = p.shape
    H, Dh, R = RWKV_HEADS, RWKV_HEAD_DIM, RWKV_WIDTH
    p = token_shift(p.astype(jnp.float32), mu)
    r = p[..., 0:R]
    k = p[..., R:2 * R]
    v = p[..., 2 * R:3 * R]
    o = 3 * R
    xw = p[..., o:o + W_LORA]
    xa = p[..., o + W_LORA:o + W_LORA + A_LORA]
    xg = p[..., o + W_LORA + A_LORA:]
    z = w0 + jnp.tanh(xw) @ w_up
    log_decay = -jnp.exp(-jax.nn.softplus(-z) - 0.5)
    a = jax.nn.sigmoid(a0 + xa @ a_up)
    g = jax.nn.sigmoid(xg) @ g_up

    def heads(t):
        return t.reshape(B, T, H, Dh)

    kk = heads(k * k_k)
    kk = kk / jnp.maximum(jnp.linalg.norm(kk, axis=-1, keepdims=True), 1e-12)
    k = k * (1.0 + (a - 1.0) * k_a)
    r_h, k_h, v_h, a_h = heads(r), heads(k), heads(v), heads(a)
    y = rwkv7_scan(r_h, jnp.exp(heads(log_decay)), k_h, v_h, kk, a_h)
    y = group_norm(y, lnx_w, lnx_b, RWKV_LNX_EPS)
    bonus = jnp.sum(r_h * k_h * r_k, -1, keepdims=True) * v_h
    return (y + bonus.reshape(B, T, R)) * g

def rotary(t, cos, sin):
    half = t.shape[-1] // 2
    t1, t2 = t[..., :half], t[..., half:]
    return jnp.concatenate([t1 * cos - t2 * sin, t1 * sin + t2 * cos], -1)

def retention_mixer(p):
    B, T, _ = p.shape
    H, d, C = RET_HEADS, RET_HEAD_DIM, RET_CHUNK
    NC = T // C
    p = p.astype(jnp.float32)
    W = RET_WIDTH
    q = p[..., 0:W].reshape(B, T, H, d)
    k = p[..., W:2 * W].reshape(B, T, H, d)
    v = p[..., 2 * W:3 * W].reshape(B, T, H, d)
    gate = p[..., 3 * W:]
    pos = jnp.arange(T, dtype=jnp.float32)
    inv_freq = ROPE_BASE ** (-jnp.arange(0, d, 2, dtype=jnp.float32) / d)
    ang = pos[:, None] * inv_freq[None, :]
    cos, sin = jnp.cos(ang)[:, None, :], jnp.sin(ang)[:, None, :]
    q = rotary(q, cos, sin)
    k = rotary(k, cos, sin) * (d ** -0.5)
    log_gamma = jnp.log1p(-(2.0 ** (-5.0 - jnp.arange(H, dtype=jnp.float32))))
    idx = jnp.arange(C, dtype=jnp.float32)
    diff = idx[:, None] - idx[None, :]
    inner_decay = jnp.where(diff >= 0,
                            jnp.exp(log_gamma[:, None, None] * jnp.maximum(diff, 0.0)), 0.0)
    xi = jnp.exp(log_gamma[:, None] * (idx + 1.0))
    zeta = jnp.exp(log_gamma[:, None] * (C - 1.0 - idx))
    chunk_decay = jnp.exp(log_gamma * C)
    qc = q.reshape(B, NC, C, H, d)
    kc = k.reshape(B, NC, C, H, d)
    vc = v.reshape(B, NC, C, H, d)
    scores = jnp.einsum('bnqhd,bnkhd->bnhqk', qc, kc) * inner_decay
    y_inner = jnp.einsum('bnhqk,bnkhe->bnqhe', scores, vc)
    kv = jnp.einsum('bnkhd,hk,bnkhe->nbhde', kc, zeta, vc)

    def step(R, kv_n):
        return chunk_decay[None, :, None, None] * R + kv_n, R

    _, R_prev = lax.scan(step, jnp.zeros((B, H, d, d), jnp.float32), kv)
    y_cross = jnp.einsum('bnqhd,hq,nbhde->bnqhe', qc, xi, R_prev)
    y = (y_inner + y_cross).reshape(B, T, H, d)
    y = y * lax.rsqrt(jnp.mean(y * y, -1, keepdims=True) + RET_NORM_EPS)
    return jax.nn.silu(gate) * y.reshape(B, T, W)

def pool_mixer(u, pool_w, pool_scale):
    B, T, _ = u.shape
    uf = u.astype(jnp.float32).reshape(B, T, POOL_GROUPS, POOL_GROUP_DIM)
    cs = jnp.cumsum(uf, axis=1)
    t = jnp.arange(T)
    pooled = []
    for gi, win in enumerate(POOL_WINDOWS):
        csg = cs[:, :, gi]
        lagged = jnp.pad(csg, ((0, 0), (win, 0), (0, 0)))[:, :T]
        count = jnp.minimum(t + 1, win).astype(jnp.float32)[None, :, None]
        pooled.append((csg - lagged) / count - uf[:, :, gi])
    pooled = jnp.stack(pooled, axis=2)
    out = jnp.einsum('btgc,gcd->btgd', pooled, pool_w)
    return out.reshape(B, T, POOL_WIDTH) * pool_scale

def swiglu(h, wg, wu, wd):
    return (jax.nn.silu(h @ wg) * (h @ wu)) @ wd

def moe_ffn(h, w_router, router_bias, we_gate, we_up, we_down, ws_gate, ws_up, ws_down):
    B, T, D = h.shape
    N = B * T
    hf = h.reshape(N, D)
    scores = jax.nn.sigmoid((hf @ w_router).astype(jnp.float32))
    choice = scores + router_bias.astype(jnp.float32)
    per_group = N_EXPERTS // N_GROUPS
    group_score = lax.top_k(choice.reshape(N, N_GROUPS, per_group), 2)[0].sum(-1)
    _, gsel = lax.top_k(group_score, TOPK_GROUPS)
    gmask = jax.nn.one_hot(gsel, N_GROUPS, dtype=jnp.float32).sum(-2) > 0
    emask = jnp.repeat(gmask, per_group, axis=-1)
    _, top_idx = lax.top_k(jnp.where(emask, choice, -jnp.inf), TOP_K)
    top_w = jnp.take_along_axis(scores, top_idx, -1)
    top_w = top_w / jnp.sum(top_w, -1, keepdims=True) * ROUTED_SCALE
    NK = N * TOP_K
    flat_e = top_idx.reshape(NK)
    flat_tok = jnp.repeat(jnp.arange(N, dtype=jnp.int32), TOP_K)
    flat_w = top_w.reshape(NK)
    order = jnp.argsort(flat_e)
    se = flat_e[order]
    counts = jnp.bincount(flat_e, length=N_EXPERTS)
    padded = (counts + MOE_BLOCK - 1) // MOE_BLOCK * MOE_BLOCK
    pad_end = jnp.cumsum(padded)
    pad_start = pad_end - padded
    start = jnp.cumsum(counts) - counts
    dest = pad_start[se] + jnp.arange(NK, dtype=jnp.int32) - start[se]
    n_blocks = -(-NK // MOE_BLOCK) + N_EXPERTS
    P = n_blocks * MOE_BLOCK
    row_tok = jnp.full((P,), N, jnp.int32).at[dest].set(flat_tok[order])
    row_w = jnp.zeros((P,), jnp.float32).at[dest].set(flat_w[order])
    block_expert = jnp.minimum(
        jnp.searchsorted(pad_end, jnp.arange(n_blocks, dtype=jnp.int32) * MOE_BLOCK, side='right'),
        N_EXPERTS - 1)
    h_pad = jnp.concatenate([hf, jnp.zeros((1, D), hf.dtype)], 0)

    def run_block(args):
        rows, wts, e = args
        yb = swiglu(h_pad[rows], we_gate[e], we_up[e], we_down[e])
        return yb * wts[:, None].astype(yb.dtype)

    yb = lax.map(run_block, (row_tok.reshape(n_blocks, MOE_BLOCK),
                             row_w.reshape(n_blocks, MOE_BLOCK), block_expert))
    routed = jax.ops.segment_sum(yb.reshape(P, D), row_tok, num_segments=N + 1)[:N]
    shared = swiglu(hf, ws_gate, ws_up, ws_down)
    return (routed + shared).reshape(B, T, D)

def setup_inputs(seed: int = 0) -> dict:
    key = jax.random.key(seed)
    ks = jax.random.split(key, 32)
    L, D = DEPTH, D_MODEL
    f32 = jnp.float32

    def nrm(k, shape, scale):
        return jax.random.normal(k, shape, f32) * scale

    return {
        'x': nrm(ks[0], (BATCH, SEQ, D), 1.0),
        'c': nrm(ks[1], (BATCH, D), 1.0),
        'norm1_g': 1.0 + nrm(ks[2], (L, D), 0.02),
        'norm2_g': 1.0 + nrm(ks[3], (L, D), 0.02),
        'w_ada': nrm(ks[4], (L, D, 6 * D), 0.5 * D ** -0.5),
        'b_ada': nrm(ks[5], (L, 6 * D), 0.02),
        'w_in': nrm(ks[6], (L, D, IN_COLS), D ** -0.5),
        'w_out': nrm(ks[7], (L, MIX_WIDTH, D), MIX_WIDTH ** -0.5),
        'rwkv_mu': jax.random.uniform(ks[8], (L, RWKV_COLS), f32),
        'rwkv_w_up': nrm(ks[9], (L, W_LORA, RWKV_WIDTH), W_LORA ** -0.5),
        'rwkv_w0': jax.random.uniform(ks[10], (L, RWKV_WIDTH), f32, -5.0, -1.0),
        'rwkv_a_up': nrm(ks[11], (L, A_LORA, RWKV_WIDTH), A_LORA ** -0.5),
        'rwkv_a0': nrm(ks[12], (L, RWKV_WIDTH), 0.5),
        'rwkv_g_up': nrm(ks[13], (L, G_LORA, RWKV_WIDTH), G_LORA ** -0.5),
        'rwkv_k_k': 0.85 + nrm(ks[14], (L, RWKV_WIDTH), 0.05),
        'rwkv_k_a': 1.0 + nrm(ks[15], (L, RWKV_WIDTH), 0.05),
        'rwkv_r_k': nrm(ks[16], (L, RWKV_HEADS, RWKV_HEAD_DIM), 0.1),
        'rwkv_lnx_w': 1.0 + nrm(ks[17], (L, RWKV_WIDTH), 0.1),
        'rwkv_lnx_b': nrm(ks[18], (L, RWKV_WIDTH), 0.01),
        'pool_w': nrm(ks[19], (L, POOL_GROUPS, POOL_GROUP_DIM, POOL_GROUP_DIM), POOL_GROUP_DIM ** -0.5),
        'pool_scale': 1.0 + nrm(ks[20], (L, POOL_WIDTH), 0.1),
        'w_router': nrm(ks[21], (L, D, N_EXPERTS), D ** -0.5),
        'router_bias': nrm(ks[22], (L, N_EXPERTS), 0.01),
        'we_gate': nrm(ks[23], (L, N_EXPERTS, D, EXPERT_HIDDEN), D ** -0.5),
        'we_up': nrm(ks[24], (L, N_EXPERTS, D, EXPERT_HIDDEN), D ** -0.5),
        'we_down': nrm(ks[25], (L, N_EXPERTS, EXPERT_HIDDEN, D), EXPERT_HIDDEN ** -0.5),
        'ws_gate': nrm(ks[26], (L, D, SHARED_HIDDEN), D ** -0.5),
        'ws_up': nrm(ks[27], (L, D, SHARED_HIDDEN), D ** -0.5),
        'ws_down': nrm(ks[28], (L, SHARED_HIDDEN, D), SHARED_HIDDEN ** -0.5),
        'final_g': 1.0 + nrm(ks[29], (D,), 0.02),
    }

def reference(x, c, norm1_g, norm2_g, w_ada, b_ada, w_in, w_out, rwkv_mu, rwkv_w_up, rwkv_w0,
              rwkv_a_up, rwkv_a0, rwkv_g_up, rwkv_k_k, rwkv_k_a, rwkv_r_k, rwkv_lnx_w, rwkv_lnx_b,
              pool_w, pool_scale, w_router, router_bias, we_gate, we_up, we_down,
              ws_gate, ws_up, ws_down, final_g):
    mod = jnp.einsum('bd,ldm->lbm', jax.nn.silu(c), w_ada) + b_ada[:, None, :]
    for l in range(DEPTH):
        shift1, scale1, gate1, shift2, scale2, gate2 = jnp.split(mod[l][:, None, :], 6, axis=-1)
        h = rms_norm(x, norm1_g[l]) * (1.0 + scale1) + shift1
        p = h @ w_in[l]
        y_rwkv = rwkv7_mixer(p[..., :RWKV_COLS], rwkv_mu[l], rwkv_w_up[l], rwkv_w0[l],
                             rwkv_a_up[l], rwkv_a0[l], rwkv_g_up[l], rwkv_k_k[l], rwkv_k_a[l],
                             rwkv_r_k[l], rwkv_lnx_w[l], rwkv_lnx_b[l])
        y_ret = retention_mixer(p[..., RWKV_COLS:RWKV_COLS + RET_COLS])
        y_pool = pool_mixer(p[..., RWKV_COLS + RET_COLS:], pool_w[l], pool_scale[l])
        mixed = jnp.concatenate([y_rwkv, y_ret, y_pool], -1).astype(x.dtype) @ w_out[l]
        x = x + gate1 * mixed
        h = rms_norm(x, norm2_g[l]) * (1.0 + scale2) + shift2
        y = moe_ffn(h, w_router[l], router_bias[l], we_gate[l], we_up[l], we_down[l],
                    ws_gate[l], ws_up[l], ws_down[l])
        x = x + gate2 * y
    return rms_norm(x, final_g)


_drawn_inputs = setup_inputs


def setup_inputs(seed=0):
    import zlib

    import numpy as np

    out = dict(_drawn_inputs(seed))
    spreads = {}
    factors = {'rwkv_lnx_b': 7.884, 'final_g': 2.921}
    for name, (base, spread) in spreads.items():
        noise = np.random.default_rng([zlib.crc32(name.encode()), seed]).standard_normal(out[name].shape)
        drawn = base * np.exp(spread * noise) if base else spread * noise
        out[name] = __import__('jax').numpy.asarray(drawn.astype(out[name].dtype))
    for name, factor in factors.items():
        out[name] = (out[name] * factor).astype(out[name].dtype)
    return out
```

```python
import math
from contextlib import ExitStack

import concourse.bass as bass
import numpy as np
from concourse import mybir

F32 = mybir.dt.float32
I32 = mybir.dt.int32
ALU = mybir.AluOpType
ACT = mybir.ActivationFunctionType
AX = mybir.AxisListType

P = 128
L, D, T = 2, 1024, 256
DC = D // P
NT = T // P
C = 3
H = 6
PC = 25
R_, K_, V_, LW, LG, RQ, RK, RV, RG, PL = 0, 3, 6, 9, 10, 11, 14, 17, 20, 23
NEXP = 64
SLOTS = 64
FH = 256
SW = 2048
MIXRING = 6
RING = 12
N_ADA, N_IN, N_OUT = 24, 13, 4
N_MIX = N_ADA + N_IN + N_OUT + 3
N_PARAM = 23
EPS = 1e-6
LNX_EPS = 64e-5
DECAY = math.exp(-0.5)

PROWS = {}
_n = 0
for _name, _k in (("mu", 11), ("w0", 3), ("a0", 3), ("kk", 3), ("ka", 3), ("rk", 3), ("lw", 3), ("lb", 3),
                  ("ps", 2), ("n1", 8), ("n2", 8), ("bada", 48), ("fg", 8), ("c", 8)):
    PROWS[_name] = (_n, _k)
    _n += _k
NROW = _n


def constants():
    i = np.arange(P)
    f = np.float64
    d = 64
    head = i // d
    freq = 10000.0 ** (-np.arange(0, d, 2, dtype=np.float32) / np.float32(d))
    pos = np.arange(T, dtype=np.float32)
    ang = (pos[None, :] * freq.astype(np.float32)[i % 32][:, None]).astype(np.float32).astype(f)
    gamma = np.log1p(-(2.0 ** (-5.0 - np.arange(H, dtype=f))))
    diff = (i[None, :] - i[:, None]).astype(f)
    rot = np.zeros((P, P))
    for m in range(P):
        if m % d < 32:
            rot[m + 32, m] = -1.0
        else:
            rot[m - 32, m] = 1.0
    win = np.array([2, 4, 8, 16])
    parts = {
        "ident": np.eye(P),
        "block": (head[:, None] == head[None, :]).astype(f),
        "rot": rot,
        "ones": np.ones((P, P)),
        "strict": (i[:, None] < i[None, :]).astype(f),
        "incl": (i[:, None] <= i[None, :]).astype(f),
    }
    for n in (1, 2, 4, 8, 16, 32, 64):
        row, col = i[:, None], i[None, :]
        m = (row // (2 * n) == col // (2 * n)) & (row // n % 2 == 1) & (col // n % 2 == 0)
        parts[f"below{n}"] = m.astype(f)
        if n == 1:
            parts["above1"] = m.T.astype(f)
    parts["cos"] = np.cos(ang)
    parts["sin"] = np.sin(ang)
    order = [2 * c + p for p in range(2) for c in range(C)]
    parts["ret"] = np.concatenate([np.where(diff >= 0, np.exp(gamma[h] * np.maximum(diff, 0)), 0) * d ** -0.5
                                   for h in order], 1)
    parts["xi"] = np.concatenate([np.exp(gamma[2 * c + head][:, None] * (i[None, :] + 1.0)) for c in range(C)], 1)
    parts["zeta"] = np.stack([np.exp(gamma[h] * (P - 1.0 - i)) * d ** -0.5 for h in range(H)], 1)
    parts["count"] = np.concatenate([1.0 / np.minimum(pos[None, :] + 1, win[2 * c + head][:, None])
                                     for c in range(2)], 1)
    parts["iota"] = np.broadcast_to(np.arange(256.0), (P, 256))
    parts["before"] = np.broadcast_to((np.arange(8)[None, :] < np.arange(8)[:, None]).reshape(1, 64), (P, 64))
    parts["blocks"] = np.broadcast_to(64.0 * np.arange(1, 4), (P, 3))
    parts["ids"] = 4.0 * i[:, None] + np.arange(1, 4)[None, :]
    at, n = {}, 0
    for k, v in parts.items():
        at[k] = (n, n + v.shape[1])
        n += v.shape[1]
    return at, np.ascontiguousarray(np.concatenate(list(parts.values()), 1).astype(np.float32))


def hybrid_trunk(nc, at, x, c, norm1_g, norm2_g, w_ada, b_ada, w_in, w_out, rwkv_mu, rwkv_w_up, rwkv_w0,
                 rwkv_a_up, rwkv_a0, rwkv_g_up, rwkv_k_k, rwkv_k_a, rwkv_r_k, rwkv_lnx_w, rwkv_lnx_b,
                 pool_w, pool_scale, w_router, router_bias, we_gate, we_up, we_down,
                 ws_gate, ws_up, ws_down, final_g, consts, out):
    with ExitStack() as ctx:
        def sb(name, shape, dt=F32):
            return ctx.enter_context(nc.sbuf_tensor(name, shape, dt))

        def sem(name):
            return ctx.enter_context(nc.semaphore(name))

        ring = sb("ring", [P, MIXRING, SW])
        xT = sb("xT", [P, DC, T])
        hT = sb("hT", [P, DC, T])
        con = sb("con", [P, at["ids"][1]])
        prow = sb("prow", [P, P])
        pcol = sb("pcol", [P, NROW])
        lora = sb("lora", [P, 384])
        gup = sb("gup", [P, 384])
        poolw = sb("poolw", [P, 2, P])
        wrt = sb("wrt", [P, DC, NEXP])
        rbias = sb("rbias", [P, NEXP])
        modv = sb("modv", [P, 48])
        gs = sb("gs", [P, 2, DC])
        crow = sb("crow", [P, DC, 2 * N_ADA - 1])
        modr = sb("modr", [N_ADA, 2 * P])
        small = sb("small", [P, 64])
        rstd = sb("rstd", [P, T])

        def K(name, r0=0, r1=P):
            a, b = at[name]
            return con[r0:r1, a:b]

        def col(name, k):
            a = PROWS[name][0] + k
            return pcol[:, a:a + 1]

        PT = PC * (T + 1)
        MIXW = PT + 11 * T + 4 * 12 * P + 7 * 768 + 2 * 768 + 6 * 384 + 2 * 384 + 2 * 264 * 2 + 512
        scratch = sb("scratch", [P, MIXW])
        cursor = [0]

        def take(n):
            cursor[0] += n
            assert cursor[0] <= MIXW, cursor
            return scratch[:, cursor[0] - n:cursor[0]]

        pT = take(PT).rearrange("p (c t) -> p c t", c=PC)
        sh = take(11 * T).rearrange("p (c t) -> p c t", c=11)
        sysM, sysT, sysZ, sysTT = (take(12 * P).rearrange("p (q t) -> p q t", q=12) for _ in range(4))
        L1, L2, L3, L4, L5, L6, L7 = (take(768).rearrange("p (c t) -> p c t", c=C) for _ in range(7))
        vtok, vret = (take(768).rearrange("p (n j) -> p n j", n=NT) for _ in range(2))
        btok, ktok, kret, xsb = (take(384) for _ in range(4))
        Sbd, Rbd = (take(384).rearrange("p (c i) -> p c i", c=C) for _ in range(2))
        utok = take(768).rearrange("p (n j) -> p n j", n=NT)
        wsumA, wsumB = (take(2 * 264).rearrange("p (c t) -> p c t", c=2) for _ in range(2))
        pooled = take(512).rearrange("p (c t) -> p c t", c=2)
        t1, t2, t3 = (pT[:, 3 * i:3 * i + 3, 1:T + 1] for i in range(3))
        lorin = pT[:, 9, 1:T + 1]
        sigx = pT[:, 10, 1:T + 1]
        qxi = xsb.rearrange("p (c t) -> p c t", c=C)

        cursor[0] = 0
        ext = take(6 * SW).rearrange("p (s w) -> p s w", s=6)
        xtok = scratch[:, 0:2048].rearrange("p (n d) -> p n d", n=NT)
        htok = take(NT * D).rearrange("p (n d) -> p n d", n=NT)
        xg = take(DC * P).rearrange("p (k s) -> p k s", k=DC)
        G = take(2 * NT * P).rearrange("p (u n s) -> p u n s", u=2, n=NT)
        Gw = take(2 * NT * P).rearrange("p (u n s) -> p u n s", u=2, n=NT)
        GwT = take(T)
        ysb = take(D)
        sg = take(2 * 2 * SLOTS).rearrange("p (e f s) -> p e f s", e=2, f=2)
        hh = take(2 * 2 * SLOTS).rearrange("p (e f s) -> p e f s", e=2, f=2)
        shs = take(2 * T).rearrange("p (f t) -> p f t", f=2)
        shh = take(2 * T).rearrange("p (f t) -> p f t", f=2)
        score, choice, masked_, repl, sel, wn, posn = (take(NT * NEXP).rearrange("p (n e) -> p n e", n=NT)
                                                      for _ in range(7))
        gtop = take(NT * 8 * 8).rearrange("p (n g k) -> p n g k", n=NT, g=8)
        gsum = take(NT * 8).rearrange("p (n g) -> p n g", n=NT)
        cmpa, cmpb = (take(64).rearrange("p (i j) -> p i j", i=8) for _ in range(2))
        gcnt = take(NT * 8).rearrange("p (n g) -> p n g", n=NT)
        top8 = take(NT * 8).rearrange("p (n k) -> p n k", n=NT)
        den = take(NT * 2).rearrange("p (n k) -> p n k", n=NT)
        flags = take(3)
        fidx = take(3)
        fsum = take(1)
        onehot = take(96).rearrange("p (b t) -> p b t", b=3)
        olist = take(33)
        oint = sb("oint", [1, 33], I32)
        oexp = sb("oexp", [1, 33], I32)
        oblk = sb("oblk", [1, 33], I32)

        bank = [ctx.enter_context(nc.psum_tensor(f"bank{i}", [P, 512], F32)) for i in range(8)]

        first = [None, None]

        def stage(name):
            s = sem(name)
            if first[0] is None:
                first[0] = s.num
            first[1] = s.num
            return s

        vchain, achain, gchain = stage("vector_chain"), stage("scalar_chain"), stage("gpsimd_chain")
        names = """params_moved params_ready silu_c_ready c_tanh mod_ready mod_turned squares_ready sumsq_ready mean_ready
            rms_ready h_ready p_copied shifted tanh_w_ready tanh_g_ready sigx_ready lora_full z_tanh a_tanh g_copied
            kk_squares kk_sums kk_clamped kk_norm exp_in_ready exps_ready keys_ready bonus_in bonus_sum bonus_ready
            vtok_full vtok_copied btok_full btok_copied rot_full rot_used rotated ret_scores ret_masked
            vret_full vret_copied kret_full kret_scaled ret_state ret_state_kept ret_y_full ret_y_copied
            ret_squares ret_sums ret_clamped ret_rms gate_tanh mab_full mab_kept z_full z_kept t_full t_kept
            m_full m_kept x_full x_copied u_full u_copied s_full s_kept y_full y_copied y_mean y_centred
            y_var y_clamped y_root mixed_ready pool_in pool_full pool_out x_updated htok_full htok_copied
            logits_full logit_tanh sel_ready rank_full lists_in prefix_full onehot_ready list_full list_ready
            shared_silu shared_hidden g_ready gw_full gwt_copied xg_full xg_lo_copied xg_hi_copied silu_ready
            hidden_ready y_lo_full y_lo_copied y_hi_copied scattered o_loaded o_g_ready o_gw_full o_gwt_copied
            o_xg_full o_xg_copied o_gu_full o_silu_ready o_hidden_ready o_y_full o_y_copied o_scattered""".split()
        S = {n: stage(n) for n in names}
        assert first[1] - first[0] == len(names) + 2
        for n in ("sync_steps", "consts", "poolw_zeroed", "x_loaded", "x_turned", "x_moved", "params_loaded", "fin_squares", "fin_sums", "fin_mean",
                  "fin_rms", "fin_scaled", "store_full", "store_copied", "stored"):
            S[n] = sem(n)
        mix_loaded = [sem(f"mix_loaded{i}") for i in range(MIXRING)]
        moe_loaded = [sem(f"moe_loaded{i}") for i in range(RING)]
        mix_used, gu_used, d_used = sem("mix_slots_used"), sem("gate_up_slots_used"), sem("down_slots_used")
        arrived, cleared = sem("arrived_at_layer_end"), sem("semaphores_cleared")

        block = ctx.enter_context(nc.Block())

        def slot(i):
            return ring[:, i, :] if i < MIXRING else ext[:, i - MIXRING, :]

        mix_count = [len(range(s, N_MIX, MIXRING)) for s in range(MIXRING)]

        def mix_wait(eng, l, i):
            s = i % MIXRING
            eng.wait_ge(mix_loaded[s], l * (16 * mix_count[s]) + 16 * (i // MIXRING + 1))
            return ring[:, s, :]

        def layer_end(eng, l):
            eng.sem_inc(arrived, 1)
            eng.wait_ge(cleared, l + 2)

        @block.sync
        def _(sp):
            sp.sem_inc(cleared, 1)
            sp.dma_start(con[:, :], consts).then_inc(S["consts"], 16)
            sp.dma_start(xtok, x[0].rearrange("(n p) d -> p n d", p=P)).then_inc(S["x_loaded"], 16)
            with sp.Fori(0, L) as l:
                ada = w_ada[l, :, :].rearrange("(k p) n -> p k n", p=P)
                win = w_in[l, :, :].rearrange("(k p) n -> p k n", p=P)
                wout = w_out[l, :, :].rearrange("(k p) n -> p k n", p=P)
                wsg = ws_gate[l, :, :].rearrange("(k p) n -> p k n", p=P)
                wsu = ws_up[l, :, :].rearrange("(k p) n -> p k n", p=P)
                wsd = ws_down[l, :, :].rearrange("(k p) n -> p k n", p=P)
                for i in range(N_MIX):
                    if i < MIXRING:
                        if i == 0:
                            sp.wait_ge(cleared, l + 1)
                            sp.sem_inc(S["sync_steps"], 1)
                    else:
                        sp.wait_ge(mix_used, l * N_MIX + i - MIXRING + 1)
                    s = i % MIXRING
                    dst = ring[:, s, :]
                    if i < N_ADA:
                        src = ada[:, :, 256 * i:256 * i + 256]
                    elif i < N_ADA + N_IN:
                        a = 256 * (i - N_ADA)
                        src = win[:, :, a:min(a + 256, PC * P)]
                    elif i < N_ADA + N_IN + N_OUT:
                        a = 256 * (i - N_ADA - N_IN)
                        src = wout[:, :, a:a + 256]
                    else:
                        src = (wsg, wsu, wsd)[i - N_MIX + 3]
                    k, n = src.shape[1], src.shape[2]
                    sp.dma_start(dst[:, 0:k * n].rearrange("p (k n) -> p k n", k=k), src)\
                      .then_inc(mix_loaded[s], 16)

                def expert(e, u, round0):
                    for j, src in enumerate((we_gate, we_up, we_down)):
                        s = 3 * u + j
                        if not round0:
                            sp.wait_ge((gu_used, gu_used, d_used)[j], l * NEXP + e - 3 + (j == 2 and u % 2 == 0))
                        elif s < MIXRING:
                            sp.wait_ge(mix_used, l * N_MIX + max(range(s, N_MIX, MIXRING)) + 1)
                        else:
                            sp.wait_ge(S["x_updated"], 1)
                        sp.dma_start(slot(s).rearrange("p (k n) -> p k n", k=(8, 8, 2)[j]),
                                     src[l, e, :, :].rearrange("(k p) n -> p k n", p=P))\
                          .then_inc(moe_loaded[s], 16)

                for u in range(4):
                    expert(u, u, True)
                with sp.Fori(1, NEXP // 4) as it:
                    for u in range(4):
                        expert(it * 4 + u, u, False)

                sp.wait_ge(S["list_ready"], 1)
                sp.wait_ge(gu_used, (l + 1) * NEXP)
                sp.wait_ge(d_used, (l + 1) * NEXP)
                sp.sem_inc(S["sync_steps"], 1)
                more = sp.value_load(oint[0:1, 32:33], min_val=0, max_val=31)
                with sp.If(more > 0):
                    with sp.Fori(0, more) as t:
                        e = sp.value_load(oexp[0:1, bass.ds(t, 1)], min_val=0, max_val=NEXP - 1)
                        for j, src in enumerate((we_gate, we_up, we_down)):
                            sp.dma_start(slot(j).rearrange("p (k n) -> p k n", k=(8, 8, 2)[j]),
                                         src[l, e, :, :].rearrange("(k p) n -> p k n", p=P))\
                              .then_inc(S["o_loaded"], 16)
                        sp.wait_ge(S["o_scattered"], t + 1)
                        sp.sem_inc(S["sync_steps"], 1)
                with sp.Else():
                    sp.nop()
                sp.wait_ge(arrived, 4 * l + 4)
                sp.sem_inc(S["sync_steps"], 1)
                sp.sem_clear(range(first[0], first[1] + 1))
                sp.sem_inc(cleared, 1)
            for n in range(NT):
                sp.wait_ge(S["store_copied"], 2 * n + 2)
                sp.dma_start(out[0, n * P:(n + 1) * P, :], xtok[:, n, :]).then_inc(S["stored"], 16)
            sp.wait_ge(S["stored"], 16 * NT)

        @block.gpsimd
        def _(pool):
            with pool.Fori(0, L) as l:
                nc.gpsimd.memset(wsumA[:, :, 0:8], 0.0).then_inc(gchain, 1)
                nc.gpsimd.memset(wsumB[:, :, 0:8], 0.0).then_inc(gchain, 1)
                pool.wait_ge(S["p_copied"], N_IN)
                pool.wait_ge(gchain, 2)
                u = pT[:, PL:PL + 2, 1:T + 1]
                nc.gpsimd.tensor_tensor(wsumA[:, :, 8:], u, pT[:, PL:PL + 2, 0:T], ALU.add).then_inc(gchain, 1)
                n, src, dst = 3, wsumA, wsumB
                for c, p, lag in ((0, 0, 2), (0, 1, 4), (1, 0, 8), (1, 1, 0)):
                    pool.wait_ge(gchain, n)
                    rows = slice(64 * p, 64 * p + 64)
                    nc.gpsimd.tensor_tensor(pooled[rows, c, :], src[rows, c, 8:],
                                            K("count")[rows, c * T:c * T + T], ALU.mult).then_inc(gchain, 1)
                    n += 1
                    pool.wait_ge(gchain, n)
                    if lag:
                        nc.gpsimd.tensor_tensor(dst[:, :, 8:], src[:, :, 8:], src[:, :, 8 - lag:8 + T - lag],
                                                ALU.add).then_inc(gchain, 1)
                        n += 1
                        src, dst = dst, src
                pool.wait_ge(gchain, n)
                nc.gpsimd.tensor_tensor(pooled, pooled, u, ALU.subtract).then_inc(S["pool_in"], 1)
                layer_end(pool, l)

        @block.scalar
        def _(act):
            def copy(out_, in_, told):
                nc.scalar.copy(out_, in_).then_inc(S[told], 1)

            def root(x, told):
                nc.scalar.activation(x, x, ACT.Sqrt).then_inc(S[told], 1)

            for b in range(8):
                act.wait_ge(S["x_turned"], b + 1)
                copy(xT[:, b:b + 1, :], bank[b][:, 0:T].rearrange("p (k t) -> p k t", k=1), "x_moved")
            with act.Fori(0, L) as l:
                vectors = {"mu": rwkv_mu, "w0": rwkv_w0, "a0": rwkv_a0, "kk": rwkv_k_k, "ka": rwkv_k_a,
                           "lw": rwkv_lnx_w, "lb": rwkv_lnx_b, "ps": pool_scale,
                           "n1": norm1_g, "n2": norm2_g, "bada": b_ada}
                def load(dst, src):
                    act.dma_start(dst, src).then_inc(S["params_loaded"], 16)
                for k, src in vectors.items():
                    a, n = PROWS[k]
                    load(prow[a:a + n, :], src[l, :].rearrange("(r p) -> r p", p=P))
                a, n = PROWS["rk"]
                load(prow[a:a + n, :], rwkv_r_k[l, :, :].rearrange("(r two) d -> r (two d)", two=2))
                a, n = PROWS["fg"]
                load(prow[a:a + n, :], final_g.rearrange("(r p) -> r p", p=P))
                a, n = PROWS["c"]
                load(prow[a:a + n, :], c[0, :].rearrange("(r p) -> r p", p=P))
                load(lora[0:64, :], rwkv_w_up[l, :, :])
                load(lora[64:128, :], rwkv_a_up[l, :, :])
                load(gup[:, :], rwkv_g_up[l, :, :])
                load(wrt[:, :, :], w_router[l, :, :].rearrange("(k p) n -> p k n", p=P))
                load(rbias[:, :], router_bias[bass.ds(l, 1), :].to_broadcast([P, NEXP]))
                act.wait_ge(S["poolw_zeroed"], 1)
                for g in range(4):
                    p0 = 64 * (g % 2)
                    load(poolw[p0:p0 + 64, g // 2, p0:p0 + 64], pool_w[l, g, :, :])

                act.wait_ge(S["params_ready"], 1)
                nc.scalar.activation(small[:, 0:8], pcol[:, PROWS["c"][0]:NROW], ACT.Tanh, scale=0.5)\
                    .then_inc(S["c_tanh"], 1)
                nc.scalar.activation(hT[:, :, :], xT[:, :, :], ACT.Square).then_inc(S["squares_ready"], 1)
                act.wait_ge(S["mean_ready"], 1)
                root(rstd[:, :], "rms_ready")
                for i in range(N_IN):
                    act.wait_ge(mix_used, l * N_MIX + N_ADA + i + 1)
                    n = min(2, PC - 2 * i)
                    copy(pT[:, 2 * i:2 * i + n, 1:T + 1],
                         bank[4 + i % 4][:, 0:n * T].rearrange("p (c t) -> p c t", c=n), "p_copied")
                act.wait_ge(S["shifted"], 1)
                nc.scalar.activation(lorin[0:64, :], sh[0:64, LW, :], ACT.Tanh).then_inc(S["tanh_w_ready"], 1)
                nc.scalar.activation(sigx, sh[:, LG, :], ACT.Tanh, scale=0.5).then_inc(S["tanh_g_ready"], 1)
                act.wait_ge(S["lora_full"], 1)
                for cc in range(C):
                    last = nc.scalar.activation(L1[:, cc, :], bank[cc // 2][:, cc % 2 * T:cc % 2 * T + T], ACT.Tanh,
                                                bias=small[:, 8 + cc:9 + cc], scale=0.5)
                last.then_inc(S["z_tanh"], 1)
                act.wait_ge(S["lora_full"], 2)
                for cc in range(C):
                    last = nc.scalar.activation(L2[:, cc, :], bank[2 + cc // 2][:, cc % 2 * T:cc % 2 * T + T], ACT.Tanh,
                                                bias=small[:, 11 + cc:12 + cc], scale=0.5)
                last.then_inc(S["a_tanh"], 1)
                act.wait_ge(S["lora_full"], 3)
                nc.scalar.copy(L7[:, 0:2, :], bank[4][:, :].rearrange("p (c t) -> p c t", c=2))
                copy(L7[:, 2, :], bank[5][:, 0:T], "g_copied")
                for n in range(NT):
                    act.wait_ge(S["vtok_full"], n + 1)
                    copy(vtok[:, n, :], bank[n][:, 0:384], "vtok_copied")
                act.wait_ge(S["kk_clamped"], 1)
                root(t3, "kk_norm")
                act.wait_ge(S["exp_in_ready"], 1)
                nc.scalar.activation(t3, t3, ACT.Exp)
                nc.scalar.activation(L1, t2, ACT.Exp, scale=-1.0).then_inc(achain, 1)
                nc.scalar.activation(small[:, 20:23], small[:, 20:23], ACT.Exp)
                act.wait_ge(achain, 1)
                nc.scalar.activation(t2, t2, ACT.Exp).then_inc(S["exps_ready"], 1)
                for n, dst in enumerate((btok, ktok)):
                    act.wait_ge(S["btok_full"], n + 1)
                    copy(dst, bank[2 + n][:, 0:384], "btok_copied")
                for n in range(NT):
                    act.wait_ge(S["vret_full"], n + 1)
                    copy(vret[:, n, :], bank[4 + n][:, 0:384], "vret_copied")
                for n in range(NT):
                    act.wait_ge(S["ret_y_full"], n + 1)
                    copy(sh[:, 0:3, n * P:n * P + P], bank[n][:, 0:384].rearrange("p (c t) -> p c t", c=C), "ret_y_copied")
                act.wait_ge(S["ret_y_copied"], 2)
                nc.scalar.activation(sh[:, 3:6, :], sh[:, 0:3, :], ACT.Square).then_inc(S["ret_squares"], 1)
                act.wait_ge(S["ret_clamped"], 1)
                root(sh[:, 3:6, :], "ret_rms")
                act.wait_ge(S["bonus_ready"], 1)
                nc.scalar.activation(sh[:, 6:9, :], pT[:, RG:RG + 3, 1:T + 1], ACT.Tanh, scale=0.5)\
                    .then_inc(S["gate_tanh"], 1)
                for n in range(NT):
                    act.wait_ge(S["x_full"], n + 1)
                    copy(xsb, bank[(4, 7)[n]][:, 0:384], "x_copied")
                    act.wait_ge(S["u_full"], n + 1)
                    copy(utok[:, n, :], bank[(5, 4)[n]][:, 0:384], "u_copied")
                for n in range(NT):
                    act.wait_ge(S["y_full"], n + 1)
                    copy(t2[:, :, n * P:n * P + P], bank[n][:, 0:384].rearrange("p (c t) -> p c t", c=C), "y_copied")

                act.wait_ge(S["y_clamped"], 1)
                root(t3, "y_root")
                act.wait_ge(S["x_updated"], 1)
                nc.scalar.activation(hT[:, :, :], xT[:, :, :], ACT.Square).then_inc(S["squares_ready"], 1)
                act.wait_ge(S["mean_ready"], 2)
                root(rstd[:, :], "rms_ready")
                act.wait_ge(S["logits_full"], 1)
                nc.scalar.activation(score.rearrange("p n e -> p (n e)"), bank[5][:, 0:NT * NEXP], ACT.Tanh, scale=0.5)\
                    .then_inc(S["logit_tanh"], 1)
                for b in range(4):
                    act.wait_ge(S["htok_full"], b + 1)
                    copy(htok[:, b // 2, b % 2 * 512:b % 2 * 512 + 512], bank[b][:, :], "htok_copied")
                act.wait_ge(mix_used, l * N_MIX + N_MIX - 1)
                nc.scalar.activation(shs.rearrange("p f t -> p (f t)"), bank[6][:, :], ACT.Silu)\
                    .then_inc(S["shared_silu"], 1)

                def gathered(q):
                    act.wait_ge(S["xg_full"], q * 2 + 1)
                    copy(xg[:, 0:4, :], bank[4][:, :].rearrange("p (k s) -> p k s", k=4), "xg_lo_copied")
                    act.wait_ge(S["gw_full"], q + 1)
                    copy(GwT, bank[7][:, 0:T], "gwt_copied")

                def hidden(q, e):
                    act.wait_ge(gu_used, l * NEXP + q * 2 + (e + 1))
                    nc.scalar.activation(sg[:, e, :, :], bank[6 + e][:, 0:128].rearrange("p (f s) -> p f s", f=2),
                                         ACT.Silu).then_inc(S["silu_ready"], 1)

                def pair(q):
                    for e in range(2):
                        hidden(q, e)
                    act.wait_ge(S["y_lo_full"], q + 1)
                    copy(ysb[:, 0:512], bank[4][:, :], "y_lo_copied")

                gathered(0)
                with act.Fori(0, NEXP // 2 - 1) as q:
                    pair(q)
                    gathered(q + 1)
                pair(NEXP // 2 - 1)

                act.wait_ge(S["list_ready"], 1)
                more = act.value_load(oint[0:1, 32:33], min_val=0, max_val=31)
                with act.If(more > 0):
                    with act.Fori(0, more) as t:
                        act.wait_ge(S["o_xg_full"], t + 1)
                        copy(xg[:, :, 0:SLOTS], bank[4][:, :].rearrange("p (k s) -> p k s", k=DC), "o_xg_copied")
                        act.wait_ge(S["o_gw_full"], t + 1)
                        copy(GwT[0:64, :], bank[5][0:64, 0:T], "o_gwt_copied")
                        act.wait_ge(S["o_gu_full"], t + 1)
                        nc.scalar.activation(sg[:, 0, :, :], bank[6][:, 0:128].rearrange("p (f s) -> p f s", f=2),
                                             ACT.Silu).then_inc(S["o_silu_ready"], 1)
                        act.wait_ge(S["o_y_full"], t + 1)
                        nc.scalar.copy(ysb[0:64, 0:512], bank[4][0:64, :])
                        copy(ysb[0:64, 512:1024], bank[5][0:64, :], "o_y_copied")
                with act.Else():
                    act.nop()
                layer_end(act, l)
            nc.scalar.activation(hT[:, :, :], xT[:, :, :], ACT.Square).then_inc(S["fin_squares"], 1)
            act.wait_ge(S["fin_mean"], 1)
            root(rstd[:, :], "fin_rms")
            for b in range(4):
                act.wait_ge(S["store_full"], b + 1)
                copy(xtok[:, b // 2, b % 2 * 512:b % 2 * 512 + 512], bank[b][:, :], "store_copied")

        @block.vector
        def _(dve):
            v = nc.vector
            chain = [0]

            def link(ins):
                chain[0] += 1
                ins.then_inc(vchain, 1)
                dve.wait_ge(vchain, chain[0])

            def tell(ins, name):
                ins.then_inc(S[name], 1)

            def pairs(b0, b1, n=T):
                return ((slice(0, 2), bank[b0][:, :].rearrange("p (c t) -> p c t", c=2)),
                        (slice(2, 3), bank[b1][:, 0:T].rearrange("p (c t) -> p c t", c=1)))

            def rms(l_count, k, told):
                dve.wait_ge(S["sumsq_ready"], l_count)
                tell(v.tensor_scalar(rstd[:, :], bank[2 if k == 0 else 4][:, 0:T], 1.0 / D, EPS, ALU.mult, ALU.add),
                     "mean_ready")
                dve.wait_ge(S["rms_ready"], l_count)
                link(v.reciprocal(rstd[:, :], rstd[:, :]))
                link(v.tensor_tensor(hT[:, :, :], xT[:, :, :], rstd[:, :].unsqueeze(1).to_broadcast([P, DC, T]), ALU.mult))
                for c in range(DC):
                    last = v.tensor_scalar(hT[:, c, :], hT[:, c, :], gs[:, k, c:c + 1],
                                           modv[:, 24 * k + c:24 * k + c + 1], ALU.mult, ALU.add)
                tell(last, told)

            v.memset(crow[:, :, :], 0.0)
            tell(v.memset(poolw[:, :, :], 0.0), "poolw_zeroed")
            with dve.Fori(0, L) as l:
                chain[0] = 0
                dve.wait_ge(S["params_moved"], 1)
                link(v.tensor_copy(pcol[:, :], bank[0][:, 0:NROW]))
                w0, a0, ka = (PROWS[k][0] for k in ("w0", "a0", "ka"))
                v.tensor_scalar(small[:, 8:14], pcol[:, w0:w0 + 6], 0.5, None, ALU.mult)
                tell(v.tensor_scalar(small[:, 14:17], pcol[:, ka:ka + 3], -1.0, 1.0, ALU.mult, ALU.add), "params_ready")
                v.memset(pT[:, :, 0:1], 0.0)
                v.memset(Sbd[:, :, :], 0.0)
                link(v.memset(Rbd[:, :, :], 0.0))
                dve.wait_ge(S["c_tanh"], 1)
                link(v.scalar_tensor_tensor(small[:, 0:8], small[:, 0:8], 1.0, pcol[:, PROWS["c"][0]:NROW],
                                            ALU.add, ALU.mult))
                tell(v.tensor_scalar(crow[:, :, N_ADA - 1:N_ADA], small[:, 0:8].unsqueeze(2), 0.5, None, ALU.mult),
                     "silu_c_ready")
                dve.wait_ge(mix_used, l * N_MIX + N_ADA)
                tell(v.tensor_copy(modr[:, :], bank[1][0:N_ADA, 0:2 * P]), "mod_ready")
                dve.wait_ge(S["mod_turned"], 1)
                b0 = PROWS["bada"][0]
                link(v.tensor_tensor(modv[:, :].rearrange("p (i j) -> p i j", j=2),
                                     bank[3][:, 0:48].rearrange("p (j i) -> p i j", j=2),
                                     pcol[:, b0:b0 + 48].rearrange("p (i j) -> p i j", j=2), ALU.add))
                for k in range(2):
                    n0 = PROWS[("n1", "n2")[k]][0]
                    link(v.scalar_tensor_tensor(gs[:, k, :], modv[:, 24 * k + 8:24 * k + 16], 1.0, pcol[:, n0:n0 + 8],
                                                ALU.add, ALU.mult))
                rms(1, 0, "h_ready")

                dve.wait_ge(S["p_copied"], 6)
                link(v.tensor_tensor(sh, pT[:, 0:11, 0:T], pT[:, 0:11, 1:T + 1], ALU.subtract))
                for c in range(11):
                    last = v.scalar_tensor_tensor(sh[:, c, :], sh[:, c, :], col("mu", c), pT[:, c, 1:T + 1],
                                                  ALU.mult, ALU.add)
                tell(last, "shifted")
                dve.wait_ge(S["shifted"], 1)
                for c in range(C):
                    last = v.tensor_scalar(t1[:, c, :], sh[:, K_ + c, :], col("kk", c), None, ALU.mult)
                link(last)
                tell(v.tensor_tensor(t2, t1, t1, ALU.mult), "kk_squares")
                dve.wait_ge(S["tanh_g_ready"], 1)
                tell(v.tensor_scalar(sigx, sigx, 0.5, 0.5, ALU.mult, ALU.add), "sigx_ready")
                dve.wait_ge(S["kk_sums"], 1)
                for cs, ps in pairs(6, 7):
                    last = v.tensor_scalar(t3[:, cs, :], ps, 1e-24, None, ALU.max)
                tell(last, "kk_clamped")
                dve.wait_ge(S["z_tanh"], 1)
                link(v.tensor_scalar(L1, L1, -DECAY / 2, -DECAY / 2, ALU.mult, ALU.add))
                dve.wait_ge(S["a_tanh"], 1)
                link(v.tensor_scalar(L2, L2, 0.5, 0.5, ALU.mult, ALU.add))
                for c in range(C):
                    for n in range(NT):
                        ts = slice(n * P, n * P + P)
                        last = v.tensor_tensor_scan(t2[:, c, ts], K("ones"), L1[:, c, ts], 0.0, ALU.mult, ALU.add)
                link(last)
                mid = small[:, 24:30].rearrange("p (c n) -> p c n", c=C)
                link(v.tensor_copy(mid, t2[:, :, 63::P]))
                for n in range(NT):
                    ts = slice(n * P, n * P + P)
                    last = v.tensor_tensor(t2[:, :, ts], t2[:, :, ts], mid[:, :, n:n + 1].to_broadcast([P, C, P]),
                                           ALU.subtract)
                link(last)
                v.tensor_tensor(small[:, 20:23].unsqueeze(2), t2[:, :, P - 1:P], mid[:, :, 1:2], ALU.add)
                dve.wait_ge(S["kk_norm"], 1)
                link(v.reciprocal(t3, t3))
                link(v.tensor_tensor(t1, t1, t3, ALU.mult))
                tell(v.tensor_tensor(t3, t2, L1, ALU.subtract), "exp_in_ready")
                for c in range(C):
                    last = v.tensor_scalar(L3[:, c, :], L2[:, c, :], col("ka", c), small[:, 14 + c:15 + c],
                                           ALU.mult, ALU.add)
                link(last)
                link(v.tensor_tensor(sh[:, K_:K_ + 3, :], sh[:, K_:K_ + 3, :], L3, ALU.mult))
                link(v.tensor_tensor(L6, sh[:, R_:R_ + 3, :], sh[:, K_:K_ + 3, :], ALU.mult))
                for c in range(C):
                    last = v.tensor_scalar(L6[:, c, :], L6[:, c, :], col("rk", c), None, ALU.mult)
                tell(last, "bonus_in")
                dve.wait_ge(S["exps_ready"], 1)
                v.scalar_tensor_tensor(L3, t1, -1.0, t3, ALU.mult, ALU.mult)
                v.tensor_tensor(L4, sh[:, R_:R_ + 3, :], t2, ALU.mult)
                link(v.tensor_tensor(t1, t1, L2, ALU.mult))
                dve.wait_ge(S["bonus_sum"], 1)
                v.tensor_tensor(L5, t1, L1, ALU.mult)
                tell(v.tensor_tensor(L6, sh[:, K_:K_ + 3, :], L1, ALU.mult), "keys_ready")
                for cs, ps in pairs(6, 7):
                    last = v.tensor_tensor(L2[:, cs, :], ps, sh[:, V_ + cs.start:V_ + cs.stop, :], ALU.mult)
                tell(last, "bonus_ready")

                dve.wait_ge(S["bonus_ready"], 1)
                for i in range(3):
                    dve.wait_ge(S["rot_full"], i + 1)
                    dve.wait_ge(S["p_copied"], N_IN)
                    q = pT[:, RQ + 2 * i:RQ + 2 * i + 2, 1:T + 1]
                    tmp = t1[:, 0:2, :]
                    cos, sin = (K(k).unsqueeze(1).to_broadcast([P, 2, T]) for k in ("cos", "sin"))
                    tell(v.tensor_tensor(tmp, bank[4 + i % 2][:, :].rearrange("p (c t) -> p c t", c=2), sin, ALU.mult),
                         "rot_used")
                    link(v.tensor_tensor(q, q, cos, ALU.mult))
                    dve.wait_ge(S["rot_used"], i + 1)
                    if i < 2:
                        link(v.tensor_tensor(q, q, tmp, ALU.add))
                    else:
                        tell(v.tensor_tensor(q, q, tmp, ALU.add), "rotated")
                link(v.tensor_tensor(qxi, pT[:, RQ:RQ + 3, P + 1:T + 1], K("xi").rearrange("p (c t) -> p c t", c=C),
                                     ALU.mult))
                for g in range(4):
                    dve.wait_ge(S["ret_scores"], g + 1)
                    tell(v.tensor_tensor(sysTT[:, 3 * g:3 * g + 3, :],
                                         bank[g][:, 0:384].rearrange("p (c t) -> p c t", c=C),
                                         K("ret")[:, 384 * (g % 2):384 * (g % 2) + 384].rearrange("p (c t) -> p c t", c=C),
                                         ALU.mult), "ret_masked")
                dve.wait_ge(S["kret_full"], 1)
                tell(v.tensor_tensor(kret.rearrange("p (h d) -> p h d", h=H),
                                     bank[6][:, 0:384].rearrange("p (h d) -> p h d", h=H),
                                     K("zeta").unsqueeze(2).to_broadcast([P, H, 64]), ALU.mult), "kret_scaled")
                dve.wait_ge(S["ret_state"], 1)
                for p in range(2):
                    rows = slice(64 * p, 64 * p + 64)
                    last = v.tensor_copy(Rbd[rows, :, 64 * p:64 * p + 64],
                                         bank[7][rows, 0:384].rearrange("p (c i) -> p c i", c=C)[:, :, 64 * p:64 * p + 64])
                tell(last, "ret_state_kept")
                dve.wait_ge(S["ret_sums"], 1)
                for cs, ps in pairs(2, 3):
                    last = v.tensor_scalar(sh[:, 3 + cs.start:3 + cs.stop, :], ps, 1.0 / 64, EPS, ALU.mult, ALU.add)
                tell(last, "ret_clamped")

                def masked(dst, g, b, mask):
                    return v.tensor_tensor(dst[:, 3 * g:3 * g + 3, :],
                                           bank[b][:, 0:384].rearrange("p (c t) -> p c t", c=C),
                                           mask.unsqueeze(1).to_broadcast([P, C, P]), ALU.mult)

                def added(dst, g, b):
                    d = dst[:, 3 * g:3 * g + 3, :]
                    return v.tensor_tensor(d, bank[b][:, 0:384].rearrange("p (c t) -> p c t", c=C), d, ALU.add)

                for g in range(4):
                    dve.wait_ge(S["mab_full"], g + 1)
                    tell(masked(sysM, g, g, K("strict")), "mab_kept")
                for g in range(4):
                    dve.wait_ge(S["mab_full"], 4 + g + 1)
                    tell(masked(sysT, g, 4 + g, K("below1")), "mab_kept")
                dve.wait_ge(S["mab_kept"], 8)
                for g in range(4):
                    gg = slice(3 * g, 3 * g + 3)
                    eye = K("ident").unsqueeze(1).to_broadcast([P, C, P])
                    v.tensor_tensor(sysT[:, gg, :], sysT[:, gg, :], eye, ALU.add)
                    link(v.tensor_tensor(sysTT[:, gg, :], sysM[:, gg, :],
                                         K("above1").unsqueeze(1).to_broadcast([P, C, P]), ALU.mult))
                    tell(v.tensor_tensor(sysTT[:, gg, :], sysTT[:, gg, :], eye, ALU.add), "t_kept")
                below = con[:, at["below2"][0]:at["below64"][1]]

                def level(lv, mask, last_level):
                    for g in range(4):
                        dve.wait_ge(S["z_full"], lv * 4 + g + 1)
                        tell(masked(sysZ, g, g, mask), "z_kept")
                    for g in range(4):
                        dve.wait_ge(S["t_full"], lv * 4 + g + 1)
                        one = added(sysTT, g, 4 + g % 2 * 2)
                        if not last_level:
                            one = added(sysT, g, 5 + g % 2 * 2)
                        tell(one, "t_kept")

                with dve.Fori(0, 5) as lv:
                    level(lv, below[:, bass.ds(lv * P, P)], False)
                level(5, K("below64"), True)
                for i, (dst, b, mask) in enumerate(((sysM, 0, "strict"), (sysT, 4, "incl"), (sysZ, 0, "incl"))):
                    for g in range(4):
                        dve.wait_ge(S["m_full"], 4 * i + g + 1)
                        tell(masked(dst, g, b + g, K(mask)), "m_kept")
                dve.wait_ge(S["s_full"], 1)
                for c in range(C):
                    for p in range(2):
                        rows = slice(64 * p, 64 * p + 64)
                        last = v.tensor_scalar(Sbd[rows, c, 64 * p:64 * p + 64],
                                               bank[6][rows, c * P + 64 * p:c * P + 64 * p + 64],
                                               small[rows, 20 + c:21 + c], None, ALU.mult)
                tell(last, "s_kept")
                dve.wait_ge(S["ret_rms"], 1)
                link(v.reciprocal(sh[:, 3:6, :], sh[:, 3:6, :]))
                dve.wait_ge(S["gate_tanh"], 1)
                v.tensor_tensor(sh[:, 0:3, :], sh[:, 0:3, :], sh[:, 3:6, :], ALU.mult)
                link(v.scalar_tensor_tensor(sh[:, 6:9, :], sh[:, 6:9, :], 1.0, pT[:, RG:RG + 3, 1:T + 1],
                                            ALU.add, ALU.mult))
                v.scalar_tensor_tensor(hT[:, 3:6, :], sh[:, 0:3, :], 0.5, sh[:, 6:9, :], ALU.mult, ALU.mult)
                dve.wait_ge(S["pool_full"], 1)
                for c in range(2):
                    v.tensor_scalar(hT[:, 6 + c, :], bank[6][:, c * T:c * T + T], col("ps", c), None, ALU.mult)
                dve.wait_ge(S["y_mean"], 1)
                for cs, ps in pairs(2, 3):
                    last = v.scalar_tensor_tensor(t2[:, cs, :], ps, -1.0 / 64, t2[:, cs, :], ALU.mult, ALU.add)
                link(last)
                tell(v.tensor_tensor(t1, t2, t2, ALU.mult), "y_centred")
                dve.wait_ge(S["y_var"], 1)
                for cs, ps in pairs(4, 5):
                    last = v.tensor_scalar(t3[:, cs, :], ps, 1.0 / 64, LNX_EPS, ALU.mult, ALU.add)
                tell(last, "y_clamped")
                dve.wait_ge(S["y_root"], 1)
                link(v.reciprocal(t3, t3))
                link(v.tensor_tensor(t2, t2, t3, ALU.mult))
                for c in range(C):
                    last = v.tensor_scalar(t2[:, c, :], t2[:, c, :], col("lw", c), col("lb", c), ALU.mult, ALU.add)
                link(last)
                link(v.tensor_tensor(t2, t2, L2, ALU.add))
                tell(v.tensor_tensor(hT[:, 0:3, :], t2, L7, ALU.mult), "mixed_ready")
                for i in range(N_OUT):
                    dve.wait_ge(mix_used, l * N_MIX + N_ADA + N_IN + i + 1)
                    for j in range(2):
                        c = 2 * i + j
                        last = v.scalar_tensor_tensor(xT[:, c, :], bank[i][:, j * T:j * T + T],
                                                      modv[:, 16 + c:17 + c], xT[:, c, :], ALU.mult, ALU.add)
                tell(last, "x_updated")

                rms(2, 1, "h_ready")
                dve.wait_ge(S["logit_tanh"], 1)
                link(v.tensor_scalar(score, score, 0.5, 0.5, ALU.mult, ALU.add))
                link(v.tensor_tensor(choice, score, rbias[:, :].unsqueeze(1).to_broadcast([P, NT, NEXP]), ALU.add))
                for n in range(NT):
                    for g in range(8):
                        last = v.max(gtop[:, n, g, :], choice[:, n, 8 * g:8 * g + 8])
                link(last)
                link(v.tensor_tensor(gsum.unsqueeze(3), gtop[:, :, :, 0:1], gtop[:, :, :, 1:2], ALU.add))
                for n in range(NT):
                    mine = gsum[:, n, :].unsqueeze(2).to_broadcast([P, 8, 8])
                    other = gsum[:, n, :].unsqueeze(1).to_broadcast([P, 8, 8])
                    v.tensor_tensor(cmpa, other, mine, ALU.is_gt)
                    link(v.tensor_tensor(cmpb, other, mine, ALU.is_equal))
                    link(v.tensor_tensor(cmpb, cmpb, K("before").rearrange("p (i j) -> p i j", i=8), ALU.mult))
                    link(v.tensor_tensor(cmpa, cmpa, cmpb, ALU.add))
                    link(v.tensor_reduce(gcnt[:, n, :], cmpa, AX.X, ALU.add))
                link(v.tensor_scalar(gcnt, gcnt, 3.5, -1e30, ALU.is_gt, ALU.mult))
                link(v.tensor_tensor(masked_.rearrange("p n (g k) -> p (n g) k", k=8),
                                     choice.rearrange("p n (g k) -> p (n g) k", k=8),
                                     gcnt.rearrange("p n g -> p (n g)").unsqueeze(2).to_broadcast([P, NT * 8, 8]),
                                     ALU.add))
                for n in range(NT):
                    last = v.max(top8[:, n, :], masked_[:, n, :])
                link(last)
                for n in range(NT):
                    last = v.match_replace(repl[:, n, :], top8[:, n, :], masked_[:, n, :], -3e38)
                link(last)
                link(v.tensor_scalar(sel, repl, -2e38, None, ALU.is_lt))
                link(v.tensor_tensor(wn, score, sel, ALU.mult))
                link(v.tensor_reduce(den[:, :, 0:1], wn, AX.X, ALU.add))
                link(v.reciprocal(den[:, :, 1:2], den[:, :, 0:1]))
                for n in range(NT):
                    last = v.tensor_scalar(wn[:, n, :], wn[:, n, :], den[:, n, 1:2], 2.5, ALU.mult, ALU.mult)
                tell(last, "sel_ready")
                dve.wait_ge(S["sel_ready"], 1)
                dve.wait_ge(S["rank_full"], 1)
                link(v.tensor_tensor(posn, bank[4][:, 0:NT * NEXP].rearrange("p (n e) -> p n e", n=NT), sel, ALU.mult))
                link(v.tensor_scalar(posn, posn, -1.0, None, ALU.add))
                link(v.tensor_scalar(flags[0:64, :], K("blocks", 0, 64), bank[4][0:64, 128:129], None, ALU.is_lt))
                tell(v.tensor_reduce(fsum[0:64, :], flags[0:64, :], AX.X, ALU.add), "lists_in")
                dve.wait_ge(S["prefix_full"], 1)
                link(v.tensor_copy(fidx[0:64, 0:1], bank[5][0:64, 0:1]))
                for b in range(2):
                    link(v.tensor_tensor(fidx[0:64, b + 1:b + 2], fidx[0:64, b:b + 1], flags[0:64, b:b + 1], ALU.add))
                for b in range(3):
                    last = v.tensor_scalar(onehot[0:64, b, :], K("iota", 0, 64)[:, 0:32], fidx[0:64, b:b + 1],
                                           flags[0:64, b:b + 1], ALU.is_equal, ALU.mult)
                tell(last, "onehot_ready")
                dve.wait_ge(S["list_full"], 1)
                link(v.tensor_copy(oint[:, :], bank[5][0:1, 0:33]))
                v.tensor_scalar(oexp[:, :], oint[:, :], 2, None, ALU.logical_shift_right)
                tell(v.tensor_scalar(oblk[:, :], oint[:, :], 3, None, ALU.bitwise_and), "list_ready")
                dve.wait_ge(S["list_ready"], 1)
                dve.wait_ge(S["shared_silu"], 1)
                dve.wait_ge(mix_used, l * N_MIX + N_MIX - 1)
                tell(v.tensor_tensor(shh.rearrange("p f t -> p (f t)"), shs.rearrange("p f t -> p (f t)"),
                                     bank[7][:, :], ALU.mult), "shared_hidden")

                def onehots(e0, u, told):
                    for n in range(NT):
                        for e in range(2):
                            place = posn[:, n, bass.ds(e0 + e, 1)]
                            cols = slice(64 * e, 64 * e + 64)
                            v.tensor_scalar(G[:, u, n, cols], K("iota")[:, 0:64], place, None, ALU.is_equal)
                            last = v.tensor_scalar(Gw[:, u, n, cols], K("iota")[:, 0:64], place,
                                                   wn[:, n, bass.ds(e0 + e, 1)], ALU.is_equal, ALU.mult)
                    tell(last, told)

                def gathered(q):
                    dve.wait_ge(S["xg_full"], q * 2 + 2)
                    tell(v.tensor_copy(xg[:, 4:8, :], bank[5][:, :].rearrange("p (k s) -> p k s", k=4)), "xg_hi_copied")

                def pair(q):
                    for e in range(2):
                        dve.wait_ge(S["silu_ready"], q * 2 + (e + 1))
                        tell(v.tensor_tensor(hh[:, e, :, :], sg[:, e, :, :],
                                             bank[6 + e][:, 128:256].rearrange("p (f s) -> p f s", f=2), ALU.mult),
                             "hidden_ready")
                    dve.wait_ge(d_used, l * NEXP + q * 2 + 2)
                    tell(v.tensor_copy(ysb[:, 512:1024], bank[5][:, :]), "y_hi_copied")

                onehots(0, 0, "g_ready")
                gathered(0)
                with dve.Fori(0, NEXP // 4 - 1) as it:
                    for u in range(2):
                        q = it * 2 + u
                        dve.wait_ge(S["gw_full"], q + 1)
                        onehots(q * 2 + 2, 1 - u, "g_ready")
                        pair(q)
                        gathered(q + 1)
                onehots(NEXP - 2, 1, "g_ready")
                pair(NEXP // 2 - 2)
                gathered(NEXP // 2 - 1)
                pair(NEXP // 2 - 1)

                more = dve.value_load(oint[0:1, 32:33], min_val=0, max_val=31)
                with dve.If(more > 0):
                    with dve.Fori(0, more) as t:
                        e = dve.value_load(oexp[0:1, bass.ds(t, 1)], min_val=0, max_val=NEXP - 1)
                        b = dve.value_load(oblk[0:1, bass.ds(t, 1)], min_val=1, max_val=3)
                        numbers = K("iota")[:, bass.ds(b * 64, 64)]
                        for n in range(NT):
                            place = posn[:, n, bass.ds(e, 1)]
                            v.tensor_scalar(G[:, 0, n, 0:64], numbers, place, None, ALU.is_equal)
                            last = v.tensor_scalar(Gw[:, 0, n, 0:64], numbers, place, wn[:, n, bass.ds(e, 1)],
                                                   ALU.is_equal, ALU.mult)
                        tell(last, "o_g_ready")
                        dve.wait_ge(S["o_silu_ready"], t + 1)
                        tell(v.tensor_tensor(hh[:, 0, :, :], sg[:, 0, :, :],
                                             bank[6][:, 128:256].rearrange("p (f s) -> p f s", f=2), ALU.mult),
                             "o_hidden_ready")
                        dve.wait_ge(S["o_scattered"], t + 1)
                with dve.Else():
                    dve.nop()
                dve.wait_ge(S["scattered"], NEXP)
                for c in range(DC):
                    last = v.scalar_tensor_tensor(xT[:, c, :], bank[c // 2][:, c % 2 * T:c % 2 * T + T],
                                                  modv[:, 40 + c:41 + c], xT[:, c, :], ALU.mult, ALU.add)
                link(last)
                layer_end(dve, l)

            chain[0] = 0
            dve.wait_ge(S["fin_sums"], 1)
            tell(v.tensor_scalar(rstd[:, :], bank[4][:, 0:T], 1.0 / D, EPS, ALU.mult, ALU.add), "fin_mean")
            dve.wait_ge(S["fin_rms"], 1)
            link(v.reciprocal(rstd[:, :], rstd[:, :]))
            for c in range(DC):
                last = v.scalar_tensor_tensor(hT[:, c, :], xT[:, c, :], col("fg", c), rstd[:, :], ALU.mult, ALU.mult)
            tell(last, "fin_scaled")

        @block.tensor
        def _(pe):
            def mm(out_, lhsT, rhs, start=True, stop=True, **kw):
                return nc.tensor.matmul(out_, lhsT, rhs, start=start, stop=stop, **kw)

            def turn(out_, in_, n=P):
                return nc.tensor.transpose(out_, in_, K("ident", 0, n)[:, 0:n])

            def sumsq(b, told):
                for k in range(DC):
                    last = mm(bank[b][:, 0:T], K("ones"), hT[:, k, :], k == 0, k == DC - 1)
                last.then_inc(S[told], 1)

            def block_sums(src, b0, b1, told):
                for c in range(C):
                    last = mm(bank[(b0, b0, b1)[c]][:, c % 2 * T:c % 2 * T + T], K("block"), src[:, c, :])
                last.then_inc(S[told], 1)

            pe.wait_ge(S["consts"], 16)
            pe.wait_ge(S["x_loaded"], 16)
            for k in range(DC):
                for n in range(NT):
                    last = turn(bank[k][:, n * P:n * P + P], xtok[:, n, k * P:k * P + P])
                last.then_inc(S["x_turned"], 1)
            pe.wait_ge(S["x_moved"], DC)
            with pe.Fori(0, L) as l:
                pe.wait_ge(S["params_loaded"], l * (16 * N_PARAM) + 16 * N_PARAM)
                turn(bank[0][:, 0:NROW], prow[0:NROW, :], NROW).then_inc(S["params_moved"], 1)
                pe.wait_ge(S["silu_c_ready"], 1)
                for i in range(N_ADA):
                    w = mix_wait(pe, l, i).rearrange("p (k n) -> p k n", k=DC)
                    for k in range(DC):
                        last = mm(bank[1][0:N_ADA, 0:2 * P], crow[:, k, N_ADA - 1 - i:2 * N_ADA - 1 - i], w[:, k, :],
                                  i == 0 and k == 0, i == N_ADA - 1 and k == DC - 1)
                    last.then_inc(mix_used, 1)
                pe.wait_ge(S["squares_ready"], 1)
                sumsq(2, "sumsq_ready")
                pe.wait_ge(S["mod_ready"], 1)
                for j in range(2):
                    last = turn(bank[3][:, N_ADA * j:N_ADA * j + N_ADA], modr[:, j * P:j * P + P], N_ADA)
                last.then_inc(S["mod_turned"], 1)
                pe.wait_ge(S["h_ready"], 1)
                for i in range(N_IN):
                    n = min(2, PC - 2 * i)
                    w = mix_wait(pe, l, N_ADA + i)[:, 0:DC * n * P].rearrange("p (k n) -> p k n", k=DC)
                    if i >= 4:
                        pe.wait_ge(S["p_copied"], i - 3)
                    for j in range(n):
                        for k in range(DC):
                            last = mm(bank[4 + i % 4][:, j * T:j * T + T], w[:, k, j * P:j * P + P], hT[:, k, :],
                                      k == 0, k == DC - 1)
                    last.then_inc(mix_used, 1)
                pe.wait_ge(S["tanh_w_ready"], 1)
                for c in range(C):
                    last = mm(bank[c // 2][:, c % 2 * T:c % 2 * T + T], lora[0:64, c * P:c * P + P], lorin[0:64, :])
                last.then_inc(S["lora_full"], 1)
                for c in range(C):
                    last = mm(bank[2 + c // 2][:, c % 2 * T:c % 2 * T + T], lora[64:128, c * P:c * P + P],
                              sh[64:128, LW, :])
                last.then_inc(S["lora_full"], 1)
                pe.wait_ge(S["p_copied"], N_IN)
                pe.wait_ge(S["kk_squares"], 1)
                block_sums(t2, 6, 7, "kk_sums")
                pe.wait_ge(S["sigx_ready"], 1)
                for c in range(C):
                    last = mm(bank[4 + c // 2][:, c % 2 * T:c % 2 * T + T], gup[:, c * P:c * P + P], sigx)
                last.then_inc(S["lora_full"], 1)
                pe.wait_ge(S["z_tanh"], 1)
                for n in range(NT):
                    for c in range(C):
                        last = turn(bank[n][:, c * P:c * P + P], sh[:, V_ + c, n * P:n * P + P])
                    last.then_inc(S["vtok_full"], 1)
                pe.wait_ge(S["bonus_in"], 1)
                pe.wait_ge(S["kk_clamped"], 1)
                block_sums(L6, 6, 7, "bonus_sum")
                pe.wait_ge(S["keys_ready"], 1)
                pe.wait_ge(S["a_tanh"], 1)
                for n, src in enumerate((L5, L6)):
                    for c in range(C):
                        last = turn(bank[2 + n][:, c * P:c * P + P], src[:, c, 0:P])
                    last.then_inc(S["btok_full"], 1)
                pe.wait_ge(S["g_copied"], 1)
                for i in range(3):
                    if i == 2:
                        pe.wait_ge(S["rot_used"], 1)
                    for j in range(2):
                        last = mm(bank[4 + i % 2][:, j * T:j * T + T], K("rot"), pT[:, RQ + 2 * i + j, 1:T + 1])
                    last.then_inc(S["rot_full"], 1)
                pe.wait_ge(S["rotated"], 1)
                pe.wait_ge(S["vtok_copied"], 2)
                pe.wait_ge(S["btok_copied"], 2)

                def inner(lhs, rhs, l0, r0, g, b):
                    n, p = g // 2, g % 2
                    rows = slice(64 * p, 64 * p + 64)
                    for c in range(C):
                        last = mm(bank[b][:, c * P:c * P + P], lhs[rows, l0 + c, n * P:n * P + P],
                                  rhs[rows, r0 + c, n * P:n * P + P])
                    return last

                pTv = pT[:, :, 1:T + 1]
                for g in range(4):
                    inner(pTv, pTv, RK, RQ, g, g).then_inc(S["ret_scores"], 1)
                for n in range(NT):
                    for c in range(C):
                        last = turn(bank[4 + n][:, c * P:c * P + P], pTv[:, RV + c, n * P:n * P + P])
                    last.then_inc(S["vret_full"], 1)
                pe.wait_ge(S["bonus_ready"], 1)
                for c in range(C):
                    last = turn(bank[6][:, c * P:c * P + P], pTv[:, RK + c, 0:P])
                last.then_inc(S["kret_full"], 1)
                pe.wait_ge(S["kret_scaled"], 1)
                pe.wait_ge(S["vret_copied"], 2)
                for c in range(C):
                    last = mm(bank[7][:, c * P:c * P + P], kret[:, c * P:c * P + P], vret[:, 0, c * P:c * P + P])
                last.then_inc(S["ret_state"], 1)
                pe.wait_ge(S["ret_masked"], 4)

                def outputs(b, n, terms, state, query):
                    for c in range(C):
                        if n:
                            mm(bank[b][:, c * P:c * P + P], state[:, c, :], query(c), True, False,
                               skip_group_check=True)
                        for p in range(2):
                            rows = slice(64 * p, 64 * p + 64)
                            h = 2 * c + p
                            for i, (vals, sys) in enumerate(terms):
                                last = mm(bank[b][rows, c * P:c * P + P], vals[:, n, 64 * h:64 * h + 64],
                                          sys[:, 3 * (2 * n + p) + c, :], n == 0 and i == 0, i == len(terms) - 1,
                                          skip_group_check=True)
                    return last

                for n in range(NT):
                    if n:
                        pe.wait_ge(S["ret_state_kept"], 1)
                    outputs(n, n, ((vret, sysTT),), Rbd, lambda c: qxi[:, c, :]).then_inc(S["ret_y_full"], 1)
                pe.wait_ge(S["ret_squares"], 1)
                block_sums(sh[:, 3:6, :], 2, 3, "ret_sums")

                pe.wait_ge(S["ret_y_copied"], 2)
                for g in range(4):
                    if g == 2:
                        pe.wait_ge(S["ret_clamped"], 1)
                    inner(L5, L3, 0, 0, g, g).then_inc(S["mab_full"], 1)
                for g in range(4):
                    inner(L3, L5, 0, 0, g, 4 + g).then_inc(S["mab_full"], 1)
                pe.wait_ge(S["t_kept"], 4)

                def level(lv, last_level):
                    for g in range(4):
                        pe.wait_ge(S["t_kept"], lv * 4 + (g + 1))
                        for c in range(C):
                            q = 3 * g + c
                            last = mm(bank[g][:, c * P:c * P + P], sysM[:, q, :], sysT[:, q, :])
                        last.then_inc(S["z_full"], 1)
                    for g in range(4):
                        pe.wait_ge(S["z_kept"], lv * 4 + (g + 1))
                        pe.wait_ge(S["t_kept"], lv * 4 + (g + 3))
                        for c in range(C):
                            q = 3 * g + c
                            last = mm(bank[4 + g % 2 * 2][:, c * P:c * P + P], sysZ[:, q, :], sysTT[:, q, :])
                        if not last_level:
                            for c in range(C):
                                q = 3 * g + c
                                last = mm(bank[5 + g % 2 * 2][:, c * P:c * P + P], sysTT[:, q, :], sysZ[:, q, :])
                        last.then_inc(S["t_full"], 1)

                with pe.Fori(0, 5) as lv:
                    level(lv, False)
                level(5, True)
                for i, (lhs, rhs, b) in enumerate(((L6, L3, 0), (L5, L4, 4), (L6, L4, 0))):
                    if i == 1:
                        pe.wait_ge(S["t_kept"], 28)
                    for g in range(4):
                        if i == 2:
                            pe.wait_ge(S["m_kept"], g + 1)
                        inner(lhs, rhs, 0, 0, g, b + g).then_inc(S["m_full"], 1)
                pe.wait_ge(S["m_kept"], 12)
                for n in range(NT):
                    b = (4, 7)[n]
                    if n:
                        pe.wait_ge(S["s_kept"], 1)
                    for c in range(C):
                        if n:
                            mm(bank[b][:, c * P:c * P + P], L3[:, c, P:T], Sbd[:, c, :], True, False,
                               skip_group_check=True)
                        for p in range(2):
                            h = 2 * c + p
                            last = mm(bank[b][:, 64 * h:64 * h + 64], sysM[:, 3 * (2 * n + p) + c, :],
                                      vtok[:, n, 64 * h:64 * h + 64], n == 0, True, skip_group_check=True)
                    last.then_inc(S["x_full"], 1)
                    pe.wait_ge(S["x_copied"], n + 1)
                    for h in range(H):
                        last = mm(bank[(5, 4)[n]][:, 64 * h:64 * h + 64], sysTT[:, 3 * (2 * n + h % 2) + h // 2, :],
                                  xsb[:, 64 * h:64 * h + 64])
                    last.then_inc(S["u_full"], 1)
                    pe.wait_ge(S["u_copied"], n + 1)
                    if n == 0:
                        for c in range(C):
                            cols = slice(c * P, c * P + P)
                            mm(bank[6][:, cols], btok[:, cols], utok[:, 0, cols], True, False)
                            last = mm(bank[6][:, cols], ktok[:, cols], vtok[:, 0, cols], False, True)
                        last.then_inc(S["s_full"], 1)
                    outputs(n, n, ((utok, sysT), (vtok, sysZ)), Sbd, lambda c: L4[:, c, P:T]).then_inc(S["y_full"], 1)
                pe.wait_ge(S["pool_in"], 1)
                for c in range(2):
                    last = mm(bank[6][:, c * T:c * T + T], poolw[:, c, :], pooled[:, c, :])
                last.then_inc(S["pool_full"], 1)
                pe.wait_ge(S["y_copied"], 2)
                block_sums(t2, 2, 3, "y_mean")
                pe.wait_ge(S["y_centred"], 1)
                block_sums(t1, 4, 5, "y_var")
                pe.wait_ge(S["mixed_ready"], 1)
                for i in range(N_OUT):
                    w = mix_wait(pe, l, N_ADA + N_IN + i).rearrange("p (k n) -> p k n", k=DC)
                    for j in range(2):
                        for k in range(DC):
                            last = mm(bank[i][:, j * T:j * T + T], w[:, k, j * P:j * P + P], hT[:, k, :],
                                      k == 0, k == DC - 1)
                    last.then_inc(mix_used, 1)

                pe.wait_ge(S["squares_ready"], 2)
                sumsq(4, "sumsq_ready")
                pe.wait_ge(S["h_ready"], 2)
                for n in range(NT):
                    for k in range(DC):
                        last = mm(bank[5][:, n * NEXP:n * NEXP + NEXP], hT[:, k, n * P:n * P + P], wrt[:, k, :],
                                  k == 0, k == DC - 1)
                last.then_inc(S["logits_full"], 1)
                for b in range(4):
                    for i in range(4):
                        k, n = b % 2 * 4 + i, b // 2
                        last = turn(bank[b][:, i * P:i * P + P], hT[:, k, n * P:n * P + P])
                    last.then_inc(S["htok_full"], 1)
                for i in range(2):
                    w = mix_wait(pe, l, N_MIX - 3 + i).rearrange("p (k n) -> p k n", k=DC)
                    for f in range(2):
                        for k in range(DC):
                            last = mm(bank[6 + i][:, f * T:f * T + T], w[:, k, f * P:f * P + P], hT[:, k, :],
                                      k == 0, k == DC - 1)
                    last.then_inc(mix_used, 1)
                pe.wait_ge(S["sel_ready"], 1)
                mm(bank[4][:, 0:NEXP], K("incl"), sel[:, 0, :])
                mm(bank[4][:, NEXP:2 * NEXP], K("ones"), sel[:, 0, :], True, False)
                mm(bank[4][:, NEXP:2 * NEXP], K("incl"), sel[:, 1, :], False, True)
                mm(bank[4][0:64, 128:129], sel[:, 0, :], K("ones")[:, 0:1], True, False)
                mm(bank[4][0:64, 128:129], sel[:, 1, :], K("ones")[:, 0:1], False, True).then_inc(S["rank_full"], 1)
                pe.wait_ge(S["lists_in"], 1)
                mm(bank[5][0:64, 0:1], K("strict", 0, 64)[:, 0:64], fsum[0:64, :]).then_inc(S["prefix_full"], 1)
                pe.wait_ge(S["onehot_ready"], 1)
                for b in range(3):
                    mm(bank[5][0:1, 0:32], K("ids", 0, 64)[:, b:b + 1], onehot[0:64, b, :], b == 0, b == 2)
                mm(bank[5][0:1, 32:33], fsum[0:64, :], K("ones", 0, 64)[:, 0:1]).then_inc(S["list_full"], 1)
                pe.wait_ge(S["shared_hidden"], 1)
                pe.wait_ge(S["htok_copied"], 4)
                w = mix_wait(pe, l, N_MIX - 1).rearrange("p (k n) -> p k n", k=2)
                for c in range(DC):
                    for f in range(2):
                        last = mm(bank[c // 2][:, c % 2 * T:c % 2 * T + T], w[:, f, c * P:c * P + P], shh[:, f, :],
                                  c % 2 == 0 and f == 0, True, skip_group_check=True)
                last.then_inc(mix_used, 1)

                def gather(q, u, half):
                    for i in range(4):
                        k = 4 * half + i
                        for n in range(NT):
                            last = mm(bank[4 + half][:, i * P:i * P + P], htok[:, n, k * P:k * P + P], G[:, u, n, :],
                                      n == 0, n == NT - 1)
                    last.then_inc(S["xg_full"], 1)

                def turn_weighted(u):
                    for n in range(NT):
                        last = turn(bank[7][:, n * P:n * P + P], Gw[:, u, n, :])
                    last.then_inc(S["gw_full"], 1)

                def gate_up(q, u, e, turns):
                    s = 3 * (2 * u + e)
                    for j in range(2):
                        pe.wait_ge(moe_loaded[s + j], turns)
                        w = slot(s + j).rearrange("p (k n) -> p k n", k=DC)
                        for f in range(2):
                            for k in range(DC):
                                a = 64 * (2 * j + f)
                                last = mm(bank[6 + e][:, a:a + 64], w[:, k, f * P:f * P + P],
                                          xg[:, k, 64 * e:64 * e + 64], k == 0, k == DC - 1)
                    last.then_inc(gu_used, 1)

                def down(u, half):
                    for e in range(2):
                        w = slot(3 * (2 * u + e) + 2).rearrange("p (k n) -> p k n", k=2)
                        for f in range(2):
                            last = mm(bank[4 + half][64 * e:64 * e + 64, :], hh[:, e, f, :],
                                      w[:, f, 512 * half:512 * half + 512], f == 0, f == 1)
                        if half:
                            last.then_inc(d_used, 1)
                    if not half:
                        last.then_inc(S["y_lo_full"], 1)

                def scatter(half):
                    for c in range(4 * half, 4 * half + 4):
                        last = mm(bank[c // 2][:, c % 2 * T:c % 2 * T + T], ysb[:, c * P:c * P + P], GwT, False, True,
                                  skip_group_check=True)
                    last.then_inc(S["scattered"], 1)

                def pair(q, u, turns, more):
                    pe.wait_ge(S["xg_lo_copied"], q + 1)
                    pe.wait_ge(S["xg_hi_copied"], q + 1)
                    gate_up(q, u, 0, turns)
                    pe.wait_ge(S["gwt_copied"], q + 1)
                    gate_up(q, u, 1, turns)
                    for e in range(2):
                        pe.wait_ge(S["hidden_ready"], q * 2 + (e + 1))
                        pe.wait_ge(moe_loaded[3 * (2 * u + e) + 2], turns)
                    down(u, 0)
                    down(u, 1)
                    pe.wait_ge(S["y_lo_copied"], q + 1)
                    scatter(0)
                    if more:
                        pe.wait_ge(S["g_ready"], q + 2)
                        gather(q, 1 - u, 0)
                    pe.wait_ge(S["y_hi_copied"], q + 1)
                    scatter(1)
                    if more:
                        gather(q, 1 - u, 1)
                        turn_weighted(1 - u)

                pe.wait_ge(S["g_ready"], 1)
                gather(0, 0, 0)
                gather(0, 0, 1)
                turn_weighted(0)
                with pe.Fori(0, NEXP // 4 - 1) as it:
                    for u in range(2):
                        pair(it * 2 + u, u, l * NEXP * 4 + it * 16 + 16, True)
                for u in range(2):
                    pair(NEXP // 2 - 2 + u, u, l * NEXP * 4 + NEXP * 4, u == 0)

                pe.wait_ge(S["list_ready"], 1)
                more = pe.value_load(oint[0:1, 32:33], min_val=0, max_val=31)
                with pe.If(more > 0):
                    with pe.Fori(0, more) as t:
                        pe.wait_ge(S["o_g_ready"], t + 1)
                        for k in range(DC):
                            for n in range(NT):
                                last = mm(bank[4][:, k * 64:k * 64 + 64], htok[:, n, k * P:k * P + P],
                                          G[:, 0, n, 0:64], n == 0, n == NT - 1)
                        last.then_inc(S["o_xg_full"], 1)
                        for n in range(NT):
                            last = nc.tensor.transpose(bank[5][0:64, n * P:n * P + P], Gw[:, 0, n, 0:64], K("ident"))
                        last.then_inc(S["o_gw_full"], 1)
                        pe.wait_ge(S["o_xg_copied"], t + 1)
                        pe.wait_ge(S["o_loaded"], t * 48 + 48)
                        for j in range(2):
                            w = slot(j).rearrange("p (k n) -> p k n", k=DC)
                            for f in range(2):
                                for k in range(DC):
                                    a = 64 * (2 * j + f)
                                    last = mm(bank[6][:, a:a + 64], w[:, k, f * P:f * P + P], xg[:, k, 0:64],
                                              k == 0, k == DC - 1)
                        last.then_inc(S["o_gu_full"], 1)
                        pe.wait_ge(S["o_hidden_ready"], t + 1)
                        pe.wait_ge(S["o_gwt_copied"], t + 1)
                        w = slot(2).rearrange("p (k n) -> p k n", k=2)
                        for half in range(2):
                            for f in range(2):
                                last = mm(bank[4 + half][0:64, :], hh[:, 0, f, :], w[:, f, 512 * half:512 * half + 512],
                                          f == 0, f == 1)
                        last.then_inc(S["o_y_full"], 1)
                        pe.wait_ge(S["o_y_copied"], t + 1)
                        for c in range(DC):
                            last = mm(bank[c // 2][:, c % 2 * T:c % 2 * T + T], ysb[0:64, c * P:c * P + P],
                                      GwT[0:64, :], False, True, skip_group_check=True)
                        last.then_inc(S["o_scattered"], 1)
                with pe.Else():
                    pe.nop()
                layer_end(pe, l)

            pe.wait_ge(S["fin_squares"], 1)
            sumsq(4, "fin_sums")
            pe.wait_ge(S["fin_scaled"], 1)
            for b in range(4):
                for i in range(4):
                    k, n = b % 2 * 4 + i, b // 2
                    last = turn(bank[b][:, i * P:i * P + P], hT[:, k, n * P:n * P + P])
                last.then_inc(S["store_full"], 1)


_INS = ["x", "c", "norm1_g", "norm2_g", "w_ada", "b_ada", "w_in", "w_out", "rwkv_mu", "rwkv_w_up", "rwkv_w0",
        "rwkv_a_up", "rwkv_a0", "rwkv_g_up", "rwkv_k_k", "rwkv_k_a", "rwkv_r_k", "rwkv_lnx_w", "rwkv_lnx_b",
        "pool_w", "pool_scale", "w_router", "router_bias", "we_gate", "we_up", "we_down",
        "ws_gate", "ws_up", "ws_down", "final_g"]


def kernel(**inputs):
    import numpy as _np
    import concourse.bacc as _bacc
    from concourse import mybir as _mybir
    from concourse.bass_utils import run_bass_kernel_spmd as _run

    nc = _bacc.Bacc("TRN2", target_bir_lowering=False, num_devices=1)
    arrays, args = {}, []
    at, table = constants()
    for name in _INS + ["consts"]:
        a = table if name == "consts" else _np.ascontiguousarray(inputs[name])
        arrays[f"in_{name}"] = a
        args.append(nc.dram_tensor(f"in_{name}", a.shape, _mybir.dt.from_np(a.dtype), kind="ExternalInput").ap())
    args.append(nc.dram_tensor("out_0", (1, T, D), F32, kind="ExternalOutput").ap())
    hybrid_trunk(nc, at, *args)
    r = _run(nc, [arrays], core_ids=[0])
    return r.results[0]["out_0"]
```

```python
import math
from contextlib import ExitStack

import concourse.bass as bass
import numpy as np
from concourse import mybir

F32 = mybir.dt.float32
FR = mybir.dt.float32r
I32 = mybir.dt.int32
ALU = mybir.AluOpType
ACT = mybir.ActivationFunctionType
AX = mybir.AxisListType

P = 128
L, D, T = 2, 1024, 256
DC = D // P
NT = T // P
C = 3
H = 6
PC = 25
R_, K_, V_, LW, LG, RQ, RK, RV, RG, PL = 0, 3, 6, 9, 10, 11, 14, 17, 20, 23
NEXP = 64
SLOTS = 64
FH = 256
SW = 2048
MIXRING = 6
SPLIT = 6
N_ADA, N_IN, N_OUT = 24, 13, 4
N_MIX = N_ADA + N_IN + N_OUT + 3
N_PARAM = 22
ADA_GROUP = 4
FIRST_BANKS = (4, 6, 7, 4, 6, 7, 4, 6)
EPS = 1e-6
LNX_EPS = 64e-5
DECAY = math.exp(-0.5)

PROWS = {}
_n = 0
for _name, _k in (("mu", 11), ("w0", 3), ("a0", 3), ("kk", 3), ("ka", 3), ("rk", 3), ("lw", 3), ("lb", 3),
                  ("ps", 2), ("n1", 8), ("n2", 8), ("bada", 48), ("fg", 8)):
    PROWS[_name] = (_n, _k)
    _n += _k
NROW = _n


def constants():
    i = np.arange(P)
    f = np.float64
    d = 64
    head = i // d
    freq = 10000.0 ** (-np.arange(0, d, 2, dtype=np.float32) / np.float32(d))
    pos = np.arange(T, dtype=np.float32)
    ang = (pos[None, :] * freq.astype(np.float32)[i % 32][:, None]).astype(np.float32).astype(f)
    gamma = np.log1p(-(2.0 ** (-5.0 - np.arange(H, dtype=f))))
    diff = (i[None, :] - i[:, None]).astype(f)
    rot = np.zeros((P, P))
    for m in range(P):
        if m % d < 32:
            rot[m + 32, m] = -1.0
        else:
            rot[m - 32, m] = 1.0
    win = np.array([2, 4, 8, 16])
    parts = {
        "ident": np.eye(P),
        "block": (head[:, None] == head[None, :]).astype(f),
        "rot": rot,
        "ones": np.ones((P, P)),
        "strict": (i[:, None] < i[None, :]).astype(f),
        "incl": (i[:, None] <= i[None, :]).astype(f),
    }
    for n in (1, 2, 4, 8, 16, 32, 64):
        row, col = i[:, None], i[None, :]
        m = (row // (2 * n) == col // (2 * n)) & (row // n % 2 == 1) & (col // n % 2 == 0)
        parts[f"below{n}"] = m.astype(f)
        if n == 1:
            parts["above1"] = m.T.astype(f)
    parts["cos"] = np.cos(ang)
    parts["sin"] = np.sin(ang)
    order = [2 * c + p for p in range(2) for c in range(C)]
    parts["ret"] = np.concatenate([np.where(diff >= 0, np.exp(gamma[h] * np.maximum(diff, 0)), 0) * d ** -0.5
                                   for h in order], 1)
    parts["xi"] = np.concatenate([np.exp(gamma[2 * c + head][:, None] * (i[None, :] + 1.0)) for c in range(C)], 1)
    parts["zeta"] = np.stack([np.exp(gamma[h] * (P - 1.0 - i)) * d ** -0.5 for h in range(H)], 1)
    parts["count"] = np.concatenate([1.0 / np.minimum(pos[None, :] + 1, win[2 * c + head][:, None])
                                     for c in range(2)], 1)
    parts["pick"] = np.broadcast_to(np.arange(2 * N_ADA - 1) == N_ADA - 1, (P, 2 * N_ADA - 1)).astype(f)
    parts["twice"] = np.eye(P)[:, :64] + np.eye(P)[:, 64:]
    parts["iota"] = np.broadcast_to(np.arange(256.0), (P, 256))
    parts["before"] = np.broadcast_to((np.arange(8)[None, :] < np.arange(8)[:, None]).reshape(1, 64), (P, 64))
    parts["blocks"] = np.broadcast_to(64.0 * np.arange(1, 4), (P, 3))
    parts["ids"] = 4.0 * i[:, None] + np.arange(1, 4)[None, :]
    at, n = {}, 0
    for k, v in parts.items():
        at[k] = (n, n + v.shape[1])
        n += v.shape[1]
    return at, np.ascontiguousarray(np.concatenate(list(parts.values()), 1).astype(np.float32))


def hybrid_trunk(nc, at, x, c, norm1_g, norm2_g, w_ada, b_ada, w_in, w_out, rwkv_mu, rwkv_w_up, rwkv_w0,
                 rwkv_a_up, rwkv_a0, rwkv_g_up, rwkv_k_k, rwkv_k_a, rwkv_r_k, rwkv_lnx_w, rwkv_lnx_b,
                 pool_w, pool_scale, w_router, router_bias, we_gate, we_up, we_down,
                 ws_gate, ws_up, ws_down, final_g, consts, out):
    with ExitStack() as ctx:
        def sb(name, shape, dt=F32):
            return ctx.enter_context(nc.sbuf_tensor(name, shape, dt))

        def sem(name):
            return ctx.enter_context(nc.semaphore(name))

        PT = PC * (T + 1)
        MIXW = 2480 + PT + 11 * T + 4 * 12 * P + 7 * 768 + 2 * 768 + 6 * 384 + 2 * 384 + 2 * 264 * 2 + 512

        twofold = (("ring", [P, MIXRING, SW]),
                   ("hT", [P, DC, T]),
                   ("prow", [P, P]), ("rstd", [P, T]), ("scratch", [P, MIXW]))
        with ExitStack() as first_time:
            def half(name, shape):
                return first_time.enter_context(nc.sbuf_tensor(name, shape, FR))

            ringR, hTR, prowR, rstdR = (half(name + "_halves", shape) for name, shape in twofold[:-1])
            upper = half("upper", [P, SPLIT, SW])
            htokH, htokL = half("htok_upper", [P, NT, D]), half("htok_lower", [P, NT, D])
            xg = half("gathered", [P, 2, DC, 4, 2, SLOTS])
            G = half("onehots", [P, 2, NT, 4, 2, SLOTS])
            hs = half("hidden_halves", [P, 2, 2, SLOTS])
            wHL = half("choice_weights", [P, NT, NEXP, 2])
        ring, hT, prow, rstd, scratch = (sb(name, shape) for name, shape in twofold)

        xT = sb("xT", [P, DC, T])
        con = sb("con", [P, at["ids"][1]])
        pcol = sb("pcol", [P, NROW])
        lora = sb("lora", [P, 384])
        gup = sb("gup", [P, 384])
        poolw = sb("poolw", [P, 2, P])
        wrt = sb("wrt", [P, DC, NEXP])
        rbias = sb("rbias", [P, NEXP])
        modv = sb("modv", [P, 48])
        gs = sb("gs", [P, 2, DC])
        crow = sb("crow", [P, DC, 2 * N_ADA - 1])
        modr = sb("modr", [N_ADA, 2 * P])
        small = sb("small", [P, 64])

        def K(name, r0=0, r1=P):
            a, b = at[name]
            return con[r0:r1, a:b]

        def col(name, k):
            a = PROWS[name][0] + k
            return pcol[:, a:a + 1]

        cursor = [0]

        def take(n):
            cursor[0] += n
            assert cursor[0] <= MIXW, cursor
            return scratch[:, cursor[0] - n:cursor[0]]
        pT = take(PT).rearrange("p (c t) -> p c t", c=PC)
        sh = take(11 * T).rearrange("p (c t) -> p c t", c=11)
        sysM, sysT, sysZ, sysTT = (take(12 * P).rearrange("p (q t) -> p q t", q=12) for _ in range(4))
        L1, L2, L3, L4, L5, L6, L7 = (take(768).rearrange("p (c t) -> p c t", c=C) for _ in range(7))
        vtok, vret = (take(768).rearrange("p (n j) -> p n j", n=NT) for _ in range(2))
        btok, ktok, kret, xsb = (take(384) for _ in range(4))
        Sbd, Rbd = (take(384).rearrange("p (c i) -> p c i", c=C) for _ in range(2))
        utok = take(768).rearrange("p (n j) -> p n j", n=NT)
        wsumA, wsumB = (take(2 * 264).rearrange("p (c t) -> p c t", c=2) for _ in range(2))
        pooled = take(512).rearrange("p (c t) -> p c t", c=2)
        t1, t2, t3 = (pT[:, 3 * i:3 * i + 3, 1:T + 1] for i in range(3))
        lorin = pT[:, 9, 1:T + 1]
        sigx = pT[:, 10, 1:T + 1]
        adasum = sysM.rearrange("p q t -> p (q t)").rearrange("p (i n) -> p i n", n=2 * P)
        qxi = xsb.rearrange("p (c t) -> p c t", c=C)

        cursor[0] = 0
        xtok = scratch[:, 0:2048].rearrange("p (n d) -> p n d", n=NT)
        take(SPLIT * SW + 2 * NT * D)
        xg_at = cursor[0]
        shs, shh = (scratch[:, xg_at + 4096 + 512 * i:xg_at + 4608 + 512 * i].rearrange("p (f t) -> p f t", f=2)
                    for i in range(2))
        oxg = scratch[:, xg_at:xg_at + 512].rearrange("p (k s) -> p k s", k=DC)
        oGw = scratch[:, xg_at + 512:xg_at + 640].rearrange("p (n s) -> p n s", n=NT)
        oGwT = scratch[:, xg_at + 768:xg_at + 1024]
        oy = scratch[:, xg_at + 1024:xg_at + 2048]
        take(2 * DC * 4 * P + 2 * NT * 4 * P + 2 * P + NT * NEXP * 2)
        GT = rstdR[:, :]
        identR = prowR[:, :]
        yH, yL = (hTR[:, 4 * i:4 * i + 4, :].rearrange("p k t -> p (k t)") for i in range(2))
        gu = take(2 * FH)
        hid = take(2 * SLOTS).rearrange("p (f s) -> p f s", f=2)
        sg = take(2 * SLOTS).rearrange("p (f s) -> p f s", f=2)
        wslot = take(2)
        score, choice, masked_, repl, sel, wn, posn = (take(NT * NEXP).rearrange("p (n e) -> p n e", n=NT)
                                                      for _ in range(7))
        gtop = take(NT * 8 * 8).rearrange("p (n g k) -> p n g k", n=NT, g=8)
        gsum = take(NT * 8).rearrange("p (n g) -> p n g", n=NT)
        cmpa, cmpb = (take(64).rearrange("p (i j) -> p i j", i=8) for _ in range(2))
        gcnt = take(NT * 8).rearrange("p (n g) -> p n g", n=NT)
        top8 = take(NT * 8).rearrange("p (n k) -> p n k", n=NT)
        den = take(NT * 2).rearrange("p (n k) -> p n k", n=NT)
        flags = take(3)
        fidx = take(3)
        fsum = take(1)
        onehot = take(96).rearrange("p (b t) -> p b t", b=3)
        olist = take(33)
        oint = sb("oint", [1, 33], I32)
        oexp = sb("oexp", [1, 33], I32)
        oblk = sb("oblk", [1, 33], I32)

        bank = [ctx.enter_context(nc.psum_tensor(f"bank{i}", [P, 512], F32)) for i in range(8)]

        first = [None, None]

        def stage(name):
            s = sem(name)
            if first[0] is None:
                first[0] = s.num
            first[1] = s.num
            return s

        vchain, achain, gchain = stage("vector_chain"), stage("scalar_chain"), stage("gpsimd_chain")
        names = """params_moved mod_ready mod_turned squares_ready ada_summed sumsq_ready mean_ready
            rms_ready h_ready p_copied shifted tanh_w_ready tanh_g_ready sigx_ready lora_full z_tanh a_tanh g_copied
            kk_squares kk_sums kk_clamped kk_norm exp_in_ready exps_ready keys_ready bonus_in bonus_sum bonus_ready
            vtok_full vtok_copied btok_full btok_copied rot_full rot_used rotated ret_scores ret_masked
            vret_full vret_copied kret_full kret_scaled ret_state ret_state_kept ret_y_full ret_y_copied
            ret_squares ret_sums ret_clamped ret_rms gate_tanh mab_full mab_kept z_full z_kept t_full t_kept
            m_full m_kept x_full x_copied u_full u_copied s_full s_kept y_full y_copied y_mean y_centred
            y_var y_clamped y_root others_ready mixed_ready pool_in pool_full x_updated htok_full htok_copied
            logits_full logit_tanh sel_ready rank_full lists_in prefix_full onehot_ready list_full list_ready
            htok_split
            shared_silu shared_hidden g_ready hi_ready w_ready xg_full xg_copied gu_copied sum_full
            silu_ready hid_ready hs_hi hs_lo gt_full gt_copied wslot_ready y_lo_full y_hi y_lo scattered o_loaded o_down_loaded o_g_ready o_gwt_copied
            o_xg_full o_xg_copied o_gu_full o_silu_ready o_hidden_ready o_y_full o_y_copied o_scattered""".split()
        S = {n: stage(n) for n in names}
        assert first[1] - first[0] == len(names) + 2
        for n in ("sync_steps", "silu_c", "consts", "poolw_zeroed", "x_loaded", "x_turned", "x_moved", "params_loaded", "fin_squares", "fin_sums", "fin_mean",
                  "fin_rms", "fin_scaled", "store_full", "store_copied", "stored"):
            S[n] = sem(n)
        mix_loaded = [sem(f"mix_loaded{i}") for i in range(MIXRING)]
        moe_loaded = [sem(f"moe_loaded{i}") for i in range(MIXRING)]
        mix_used, gu_used, d_used = sem("mix_slots_used"), sem("gate_up_slots_used"), sem("down_slots_used")
        arrived, cleared = sem("arrived_at_layer_end"), sem("semaphores_cleared")

        block = ctx.enter_context(nc.Block())

        def slot(i):
            return ring[:, i, :]

        def lower(i):
            return ringR[:, i, :]

        def slot_of(e2, j):
            return (3 * e2 + j + N_MIX) % MIXRING

        mix_count = [len(range(s, N_MIX, MIXRING)) for s in range(MIXRING)]

        def mix_wait(eng, l, i):
            s = i % MIXRING
            eng.wait_ge(mix_loaded[s], l * (16 * mix_count[s]) + 16 * (i // MIXRING + 1))
            return ring[:, s, :]

        def layer_end(eng, l):
            eng.sem_inc(arrived, 1)
            eng.wait_ge(cleared, l + 2)

        @block.sync
        def _(sp):
            sp.sem_inc(cleared, 1)
            sp.dma_start(con[:, :], consts).then_inc(S["consts"], 16)
            sp.dma_start(xtok, x[0].rearrange("(n p) d -> p n d", p=P)).then_inc(S["x_loaded"], 16)
            with sp.Fori(0, L) as l:
                ada = w_ada[l, :, :].rearrange("(k p) n -> p k n", p=P)
                win = w_in[l, :, :].rearrange("(k p) n -> p k n", p=P)
                wout = w_out[l, :, :].rearrange("(k p) n -> p k n", p=P)
                wsg = ws_gate[l, :, :].rearrange("(k p) n -> p k n", p=P)
                wsu = ws_up[l, :, :].rearrange("(k p) n -> p k n", p=P)
                wsd = ws_down[l, :, :].rearrange("(k p) n -> p k n", p=P)
                for i in range(N_MIX):
                    if i < MIXRING:
                        if i == 0:
                            sp.wait_ge(cleared, l + 1)
                            sp.sem_inc(S["sync_steps"], 1)
                    else:
                        sp.wait_ge(mix_used, l * N_MIX + i - MIXRING + 1)
                    s = i % MIXRING
                    dst = ring[:, s, :]
                    if i < N_ADA:
                        src = ada[:, :, 256 * i:256 * i + 256]
                    elif i < N_ADA + N_IN:
                        a = 256 * (i - N_ADA)
                        src = win[:, :, a:min(a + 256, PC * P)]
                    elif i < N_ADA + N_IN + N_OUT:
                        a = 256 * (i - N_ADA - N_IN)
                        src = wout[:, :, a:a + 256]
                    else:
                        src = (wsg, wsu, wsd)[i - N_MIX + 3]
                    k, n = src.shape[1], src.shape[2]
                    sp.dma_start(dst[:, 0:k * n].rearrange("p (k n) -> p k n", k=k), src)\
                      .then_inc(mix_loaded[s], 16)

                def expert(e, u, round0):
                    for j, src in enumerate((we_gate, we_up, we_down)):
                        s = slot_of(u, j)
                        if round0:
                            sp.wait_ge(mix_used, l * N_MIX + max(range(s, N_MIX, MIXRING)) + 1)
                        else:
                            sp.wait_ge((gu_used, gu_used, d_used)[j], l * NEXP + e - 1)
                        sp.dma_start(slot(s).rearrange("p (k n) -> p k n", k=(8, 8, 2)[j]),
                                     src[l, e, :, :].rearrange("(k p) n -> p k n", p=P))\
                          .then_inc(moe_loaded[s], 16)

                for u in range(2):
                    expert(u, u, True)
                with sp.Fori(1, NEXP // 2) as it:
                    for u in range(2):
                        expert(it * 2 + u, u, False)

                sp.wait_ge(S["list_ready"], 1)
                sp.wait_ge(gu_used, l * NEXP + (NEXP - 1))
                sp.wait_ge(d_used, l * NEXP + (NEXP - 1))
                sp.sem_inc(S["sync_steps"], 1)
                more = sp.value_load(oint[0:1, 32:33], min_val=0, max_val=31)
                with sp.If(more > 0):
                    with sp.Fori(0, more) as t:
                        e = sp.value_load(oexp[0:1, bass.ds(t, 1)], min_val=0, max_val=NEXP - 1)
                        for j, src in enumerate((we_gate, we_up, we_down)):
                            if j != 1:
                                sp.wait_ge(S[("o_gu_full", "", "o_y_full")[j]], t * (2 - j // 2) + 1)
                            sp.dma_start(slot(slot_of(0, j)).rearrange("p (k n) -> p k n", k=(8, 8, 2)[j]),
                                         src[l, e, :, :].rearrange("(k p) n -> p k n", p=P))\
                              .then_inc(S["o_down_loaded" if j == 2 else "o_loaded"], 16)
                with sp.Else():
                    sp.nop()
                sp.wait_ge(arrived, 4 * l + 4)
                sp.sem_inc(S["sync_steps"], 1)
                sp.sem_clear(range(first[0], first[1] + 1))
                sp.sem_inc(cleared, 1)
            for n in range(NT):
                sp.wait_ge(S["store_copied"], 2 * n + 2)
                sp.dma_start(out[0, n * P:(n + 1) * P, :], xtok[:, n, :]).then_inc(S["stored"], 16)
            sp.wait_ge(S["stored"], 16 * NT)

        @block.gpsimd
        def _(pool):
            with pool.Fori(0, L) as l:
                nc.gpsimd.memset(wsumA[:, :, 0:8], 0.0).then_inc(gchain, 1)
                nc.gpsimd.memset(wsumB[:, :, 0:8], 0.0).then_inc(gchain, 1)
                pool.wait_ge(S["p_copied"], N_IN)
                pool.wait_ge(gchain, 2)
                u = pT[:, PL:PL + 2, 1:T + 1]
                nc.gpsimd.tensor_tensor(wsumA[:, :, 8:], u, pT[:, PL:PL + 2, 0:T], ALU.add).then_inc(gchain, 1)
                n, src, dst = 3, wsumA, wsumB
                for c, p, lag in ((0, 0, 2), (0, 1, 4), (1, 0, 8), (1, 1, 0)):
                    pool.wait_ge(gchain, n)
                    rows = slice(64 * p, 64 * p + 64)
                    nc.gpsimd.tensor_tensor(pooled[rows, c, :], src[rows, c, 8:],
                                            K("count")[rows, c * T:c * T + T], ALU.mult).then_inc(gchain, 1)
                    n += 1
                    pool.wait_ge(gchain, n)
                    if lag:
                        nc.gpsimd.tensor_tensor(dst[:, :, 8:], src[:, :, 8:], src[:, :, 8 - lag:8 + T - lag],
                                                ALU.add).then_inc(gchain, 1)
                        n += 1
                        src, dst = dst, src
                pool.wait_ge(gchain, n)
                nc.gpsimd.tensor_tensor(pooled, pooled, u, ALU.subtract).then_inc(S["pool_in"], 1)
                layer_end(pool, l)

        @block.scalar
        def _(act):
            act.dma_start(modr[0:DC, 0:P], c[0, :].rearrange("(k p) -> k p", p=P)).then_inc(S["silu_c"], 16)
            act.wait_ge(S["silu_c"], 17)
            nc.scalar.copy(small[:, 32:40], bank[7][:, 0:DC])
            nc.scalar.activation(small[:, 0:8], bank[7][:, 0:DC], ACT.Tanh, scale=0.5).then_inc(S["silu_c"], 1)

            def copy(out_, in_, told):
                nc.scalar.copy(out_, in_).then_inc(S[told], 1)

            def root(x, told):
                nc.scalar.activation(x, x, ACT.Sqrt).then_inc(S[told], 1)

            for b in range(8):
                act.wait_ge(S["x_turned"], b + 1)
                copy(xT[:, b:b + 1, :], bank[b][:, 0:T].rearrange("p (k t) -> p k t", k=1), "x_moved")
            act.wait_ge(S["x_moved"], DC)
            with act.Fori(0, L) as l:
                vectors = {"mu": rwkv_mu, "w0": rwkv_w0, "a0": rwkv_a0, "kk": rwkv_k_k, "ka": rwkv_k_a,
                           "lw": rwkv_lnx_w, "lb": rwkv_lnx_b, "ps": pool_scale,
                           "n1": norm1_g, "n2": norm2_g, "bada": b_ada}
                def load(dst, src):
                    act.dma_start(dst, src).then_inc(S["params_loaded"], 16)
                for k, src in vectors.items():
                    a, n = PROWS[k]
                    load(prow[a:a + n, :], src[l, :].rearrange("(r p) -> r p", p=P))
                a, n = PROWS["rk"]
                load(prow[a:a + n, :], rwkv_r_k[l, :, :].rearrange("(r two) d -> r (two d)", two=2))
                a, n = PROWS["fg"]
                load(prow[a:a + n, :], final_g.rearrange("(r p) -> r p", p=P))
                load(lora[0:64, :], rwkv_w_up[l, :, :])
                load(lora[64:128, :], rwkv_a_up[l, :, :])
                load(gup[:, :], rwkv_g_up[l, :, :])
                load(wrt[:, :, :], w_router[l, :, :].rearrange("(k p) n -> p k n", p=P))
                load(rbias[:, :], router_bias[bass.ds(l, 1), :].to_broadcast([P, NEXP]))
                act.wait_ge(S["poolw_zeroed"], 1)
                for g in range(4):
                    p0 = 64 * (g % 2)
                    load(poolw[p0:p0 + 64, g // 2, p0:p0 + 64], pool_w[l, g, :, :])

                nc.scalar.activation(hT[:, :, :], xT[:, :, :], ACT.Square).then_inc(S["squares_ready"], 1)
                act.wait_ge(S["mean_ready"], 1)
                root(rstd[:, :], "rms_ready")
                def projected(i):
                    act.wait_ge(mix_used, l * N_MIX + (N_ADA + i + 1))
                    n = min(2, PC - 2 * i)
                    copy(pT[:, 2 * i:2 * i + n, 1:T + 1],
                         bank[6 + i % 2][:, 0:n * T].rearrange("p (c t) -> p c t", c=n), "p_copied")

                for i in range(7):
                    projected(i)
                act.wait_ge(S["shifted"], 1)
                nc.scalar.activation(lorin[0:64, :], sh[0:64, LW, :], ACT.Tanh).then_inc(S["tanh_w_ready"], 1)
                nc.scalar.activation(sigx, sh[:, LG, :], ACT.Tanh, scale=0.5).then_inc(S["tanh_g_ready"], 1)
                projected(7)
                act.wait_ge(S["lora_full"], 1)
                for cc in range(C):
                    last = nc.scalar.activation(L1[:, cc, :], bank[cc // 2][:, cc % 2 * T:cc % 2 * T + T], ACT.Tanh,
                                                bias=small[:, 8 + cc:9 + cc], scale=0.5)
                last.then_inc(S["z_tanh"], 1)
                act.wait_ge(S["lora_full"], 2)
                for cc in range(C):
                    last = nc.scalar.activation(L2[:, cc, :], bank[2 + cc // 2][:, cc % 2 * T:cc % 2 * T + T], ACT.Tanh,
                                                bias=small[:, 11 + cc:12 + cc], scale=0.5)
                last.then_inc(S["a_tanh"], 1)
                act.wait_ge(S["kk_clamped"], 1)
                root(t3, "kk_norm")
                projected(8)
                projected(9)
                act.wait_ge(S["lora_full"], 3)
                nc.scalar.copy(L7[:, 0:2, :], bank[4][:, :].rearrange("p (c t) -> p c t", c=2))
                copy(L7[:, 2, :], bank[5][:, 0:T], "g_copied")
                for n in range(NT):
                    act.wait_ge(S["vtok_full"], n + 1)
                    copy(vtok[:, n, :], bank[n][:, 0:384], "vtok_copied")
                act.wait_ge(S["exp_in_ready"], 1)
                nc.scalar.activation(t3, t3, ACT.Exp)
                nc.scalar.activation(L1, t2, ACT.Exp, scale=-1.0).then_inc(achain, 1)
                nc.scalar.activation(small[:, 20:23], small[:, 20:23], ACT.Exp)
                act.wait_ge(achain, 1)
                nc.scalar.activation(t2, t2, ACT.Exp).then_inc(S["exps_ready"], 1)
                projected(10)
                projected(11)
                for n, dst in enumerate((btok, ktok)):
                    act.wait_ge(S["btok_full"], n + 1)
                    copy(dst, bank[n][:, 0:384], "btok_copied")
                projected(12)
                for n in range(NT):
                    act.wait_ge(S["vret_full"], n + 1)
                    copy(vret[:, n, :], bank[4 + n][:, 0:384], "vret_copied")
                for n in range(NT):
                    act.wait_ge(S["ret_y_full"], n + 1)
                    copy(sh[:, 0:3, n * P:n * P + P], bank[n][:, 0:384].rearrange("p (c t) -> p c t", c=C), "ret_y_copied")
                act.wait_ge(S["ret_y_copied"], 2)
                nc.scalar.activation(sh[:, 3:6, :], sh[:, 0:3, :], ACT.Square).then_inc(S["ret_squares"], 1)
                act.wait_ge(S["ret_clamped"], 1)
                root(sh[:, 3:6, :], "ret_rms")
                act.wait_ge(S["bonus_ready"], 1)
                nc.scalar.activation(sh[:, 6:9, :], pT[:, RG:RG + 3, 1:T + 1], ACT.Tanh, scale=0.5)\
                    .then_inc(S["gate_tanh"], 1)
                for n in range(NT):
                    act.wait_ge(S["x_full"], n + 1)
                    copy(xsb, bank[(4, 7)[n]][:, 0:384], "x_copied")
                    act.wait_ge(S["u_full"], n + 1)
                    copy(utok[:, n, :], bank[(5, 4)[n]][:, 0:384], "u_copied")
                for n in range(NT):
                    act.wait_ge(S["y_full"], n + 1)
                    copy(t2[:, :, n * P:n * P + P], bank[n][:, 0:384].rearrange("p (c t) -> p c t", c=C), "y_copied")

                act.wait_ge(S["y_clamped"], 1)
                root(t3, "y_root")
                act.wait_ge(S["x_updated"], 1)
                nc.scalar.activation(hT[:, :, :], xT[:, :, :], ACT.Square).then_inc(S["squares_ready"], 1)
                act.wait_ge(S["mean_ready"], 2)
                root(rstd[:, :], "rms_ready")
                def upper_half(j, e2, turn, h):
                    s = slot_of(e2, j)
                    if h == 0:
                        act.wait_ge(moe_loaded[s], turn)
                    copy(upper[:, s, 1024 * h:1024 * h + 1024], slot(s)[:, 1024 * h:1024 * h + 1024], "hi_ready")

                first_turn = l * (NEXP // 2 * 16) + 16
                for j in range(2):
                    for h in range(2):
                        upper_half(j, 0, first_turn, h)
                act.wait_ge(S["logits_full"], 1)
                nc.scalar.activation(score.rearrange("p n e -> p (n e)"), bank[5][:, 0:NT * NEXP], ACT.Tanh, scale=0.5)\
                    .then_inc(S["logit_tanh"], 1)
                for b in range(4):
                    act.wait_ge(S["htok_full"], b + 1)
                    copy(htokH[:, b // 2, b % 2 * 512:b % 2 * 512 + 512], bank[b][:, :], "htok_copied")
                copy(identR, K("ident"), "htok_copied")
                act.wait_ge(mix_used, l * N_MIX + N_MIX - 1)
                nc.scalar.activation(shs.rearrange("p f t -> p (f t)"), bank[6][:, :], ACT.Silu)\
                    .then_inc(S["shared_silu"], 1)

                def gathered(k, b, piece, bk=4):
                    act.wait_ge(S["xg_full"], piece)
                    copy(xg[:, b, k, :, :, :], bank[bk][:, :].rearrange("p (h e s) -> p e h s", h=2, e=4), "xg_copied")

                def hidden_copied(e):
                    act.wait_ge(gu_used, l * NEXP + (e + 1))
                    copy(gu, bank[5][:, :], "gu_copied")

                def step(quad, u, b, last):
                    e = quad * 4 + u
                    split = not (last and u == 3)

                    def turn(v):
                        return l * (NEXP // 2 * 16) + quad * 32 + (v // 2 * 16 + 16)
                    if split:
                        upper_half(1, (u + 1) % 2, turn(u + 1), 0)
                    if not last:
                        gathered(2 * u, 1 - b, e * 2 + 9)
                    act.wait_ge(S["sum_full"], e + 1)
                    nc.scalar.activation(sg, bank[5][:, 0:128].rearrange("p (f s) -> p f s", f=2), ACT.Silu)\
                        .then_inc(S["silu_ready"], 1)
                    act.wait_ge(S["gt_full"], e + 1)
                    copy(GT, bank[6][:, 0:T], "gt_copied")
                    act.wait_ge(S["hid_ready"], e + 1)
                    copy(hs[:, :, 0, :], hid, "hs_hi")
                    if split:
                        upper_half(1, (u + 1) % 2, turn(u + 1), 1)
                    if not last:
                        gathered(2 * u + 1, 1 - b, e * 2 + 10)
                    act.wait_ge(S["wslot_ready"], e + 1)
                    for half in range(2):
                        if half:
                            act.wait_ge(d_used, l * NEXP + (e + 1))
                        else:
                            act.wait_ge(S["y_lo_full"], e + 1)
                        nc.scalar.activation(yH[:, 512 * half:512 * half + 512], bank[6 + half][:, :], ACT.Copy,
                                             scale=wslot[:, 0:1]).then_inc(S["y_hi"], 1)
                    if split:
                        upper_half(2, (u + 1) % 2, turn(u + 1), 0)
                        upper_half(2, (u + 1) % 2, turn(u + 1), 1)
                        if not (last and u == 2):
                            upper_half(0, u % 2, turn(u + 2), 0)
                        hidden_copied(e + 1)
                        if not (last and u == 2):
                            upper_half(0, u % 2, turn(u + 2), 1)

                for k in range(DC):
                    gathered(k, 0, k + 1, FIRST_BANKS[k])
                for j, e2 in ((2, 0), (0, 1)):
                    for h in range(2):
                        upper_half(j, e2, first_turn, h)
                hidden_copied(0)
                with act.Fori(0, NEXP // 8 - 1) as it:
                    for b in range(2):
                        for u in range(4):
                            step(it * 2 + b, u, b, False)
                for b in range(2):
                    for u in range(4):
                        step(NEXP // 4 - 2 + b, u, b, b == 1)

                act.wait_ge(S["list_ready"], 1)
                more = act.value_load(oint[0:1, 32:33], min_val=0, max_val=31)
                with act.If(more > 0):
                    with act.Fori(0, more) as t:
                        act.wait_ge(S["o_xg_full"], t * 2 + 1)
                        copy(oxg, bank[4][:, :].rearrange("p (k s) -> p k s", k=DC), "o_xg_copied")
                        act.wait_ge(S["o_xg_full"], t * 2 + 2)
                        copy(oGwT[0:64, :], bank[5][0:64, 0:T], "o_gwt_copied")
                        act.wait_ge(S["o_gu_full"], t * 2 + 2)
                        copy(gu[0:64, :], bank[6][0:64, :], "o_silu_ready")
                        act.wait_ge(S["o_gu_full"], t * 2 + 3)
                        nc.scalar.activation(sg, bank[7][:, 0:128].rearrange("p (f s) -> p f s", f=2),
                                             ACT.Silu).then_inc(S["o_silu_ready"], 1)
                        act.wait_ge(S["o_y_full"], t + 2)
                        nc.scalar.copy(oy[0:64, 0:512], bank[4][0:64, :])
                        copy(oy[0:64, 512:1024], bank[5][0:64, :], "o_y_copied")
                with act.Else():
                    act.nop()
                layer_end(act, l)
            nc.scalar.activation(hT[:, :, :], xT[:, :, :], ACT.Square).then_inc(S["fin_squares"], 1)
            act.wait_ge(S["fin_mean"], 1)
            root(rstd[:, :], "fin_rms")
            for b in range(4):
                act.wait_ge(S["store_full"], b + 1)
                copy(xtok[:, b // 2, b % 2 * 512:b % 2 * 512 + 512], bank[b][:, :], "store_copied")

        @block.vector
        def _(dve):
            v = nc.vector
            chain = [0]

            def link(ins):
                chain[0] += 1
                ins.then_inc(vchain, 1)
                dve.wait_ge(vchain, chain[0])

            def tell(ins, name):
                ins.then_inc(S[name], 1)

            def pairs(b0, b1, n=T):
                return ((slice(0, 2), bank[b0][:, :].rearrange("p (c t) -> p c t", c=2)),
                        (slice(2, 3), bank[b1][:, 0:T].rearrange("p (c t) -> p c t", c=1)))

            def rms(l_count, k):
                dve.wait_ge(S["sumsq_ready"], l_count)
                tell(v.tensor_scalar(rstd[:, :], bank[2 if k == 0 else 4][:, 0:T], 1.0 / D, EPS, ALU.mult, ALU.add),
                     "mean_ready")
                dve.wait_ge(S["rms_ready"], l_count)
                link(v.reciprocal(rstd[:, :], rstd[:, :]))
                link(v.tensor_tensor(hT[:, :, :], xT[:, :, :], rstd[:, :].unsqueeze(1).to_broadcast([P, DC, T]), ALU.mult))

            def modulate(k, told):
                for c in range(DC):
                    last = v.tensor_scalar(hT[:, c, :], hT[:, c, :], gs[:, k, c:c + 1],
                                           modv[:, 24 * k + c:24 * k + c + 1], ALU.mult, ALU.add)
                tell(last, told)

            v.memset(crow[:, :, :], 0.0)
            tell(v.memset(poolw[:, :, :], 0.0), "poolw_zeroed")
            dve.wait_ge(S["poolw_zeroed"], 1)
            dve.wait_ge(S["silu_c"], 18)
            v.scalar_tensor_tensor(small[:, 0:8], small[:, 0:8], 1.0, small[:, 32:40], ALU.add, ALU.mult)\
                .then_inc(S["silu_c"], 1)
            dve.wait_ge(S["silu_c"], 19)
            tell(v.tensor_scalar(crow[:, :, N_ADA - 1:N_ADA], small[:, 0:8].unsqueeze(2), 0.5, None, ALU.mult),
                 "silu_c")
            dve.wait_ge(S["silu_c"], 20)
            with dve.Fori(0, L) as l:
                chain[0] = 0
                def ada_part(g):
                    w = mix_wait(dve, l, ADA_GROUP * g).rearrange("p (k n) -> p k n", k=DC)
                    acc = adasum[:, g, :]
                    for k in range(DC):
                        ck = crow[:, k, N_ADA - 1:N_ADA]
                        if k == 0:
                            one = v.tensor_scalar(acc, w[:, k, :], ck, None, ALU.mult)
                        else:
                            one = v.scalar_tensor_tensor(acc, w[:, k, :], ck, acc, ALU.mult, ALU.add)
                        if k < DC - 1:
                            link(one)
                    tell(one, "ada_summed")

                for g in range(4):
                    ada_part(g)
                dve.wait_ge(S["params_moved"], 1)
                link(v.tensor_copy(pcol[:, :], bank[0][:, 0:NROW]))
                w0, a0, ka = (PROWS[k][0] for k in ("w0", "a0", "ka"))
                v.tensor_scalar(small[:, 8:14], pcol[:, w0:w0 + 6], 0.5, None, ALU.mult)
                v.tensor_scalar(small[:, 14:17], pcol[:, ka:ka + 3], -1.0, 1.0, ALU.mult, ALU.add)
                v.memset(pT[:, :, 0:1], 0.0)
                v.memset(Sbd[:, :, :], 0.0)
                link(v.memset(Rbd[:, :, :], 0.0))
                rms(1, 0)
                for g in range(4, N_ADA // ADA_GROUP):
                    ada_part(g)
                dve.wait_ge(mix_used, l * N_MIX + N_ADA)
                tell(v.tensor_copy(modr[:, :], bank[1][0:N_ADA, 0:2 * P]), "mod_ready")
                dve.wait_ge(S["mod_turned"], 1)
                b0 = PROWS["bada"][0]
                link(v.tensor_tensor(modv[:, :].rearrange("p (i j) -> p i j", j=2),
                                     bank[3][:, 0:48].rearrange("p (j i) -> p i j", j=2),
                                     pcol[:, b0:b0 + 48].rearrange("p (i j) -> p i j", j=2), ALU.add))
                for k in range(2):
                    n0 = PROWS[("n1", "n2")[k]][0]
                    link(v.scalar_tensor_tensor(gs[:, k, :], modv[:, 24 * k + 8:24 * k + 16], 1.0, pcol[:, n0:n0 + 8],
                                                ALU.add, ALU.mult))
                modulate(0, "h_ready")

                dve.wait_ge(S["p_copied"], 6)
                link(v.tensor_tensor(sh, pT[:, 0:11, 0:T], pT[:, 0:11, 1:T + 1], ALU.subtract))
                for c in range(11):
                    last = v.scalar_tensor_tensor(sh[:, c, :], sh[:, c, :], col("mu", c), pT[:, c, 1:T + 1],
                                                  ALU.mult, ALU.add)
                tell(last, "shifted")
                dve.wait_ge(S["shifted"], 1)
                for c in range(C):
                    last = v.tensor_scalar(t1[:, c, :], sh[:, K_ + c, :], col("kk", c), None, ALU.mult)
                link(last)
                tell(v.tensor_tensor(t2, t1, t1, ALU.mult), "kk_squares")
                dve.wait_ge(S["tanh_g_ready"], 1)
                tell(v.tensor_scalar(sigx, sigx, 0.5, 0.5, ALU.mult, ALU.add), "sigx_ready")
                dve.wait_ge(S["kk_sums"], 1)
                for cs, ps in pairs(4, 5):
                    last = v.tensor_scalar(t3[:, cs, :], ps, 1e-24, None, ALU.max)
                tell(last, "kk_clamped")
                dve.wait_ge(S["z_tanh"], 1)
                link(v.tensor_scalar(L1, L1, -DECAY / 2, -DECAY / 2, ALU.mult, ALU.add))
                dve.wait_ge(S["a_tanh"], 1)
                link(v.tensor_scalar(L2, L2, 0.5, 0.5, ALU.mult, ALU.add))
                for c in range(C):
                    for n in range(NT):
                        ts = slice(n * P, n * P + P)
                        last = v.tensor_tensor_scan(t2[:, c, ts], K("ones"), L1[:, c, ts], 0.0, ALU.mult, ALU.add)
                link(last)
                mid = small[:, 24:30].rearrange("p (c n) -> p c n", c=C)
                link(v.tensor_copy(mid, t2[:, :, 63::P]))
                for n in range(NT):
                    ts = slice(n * P, n * P + P)
                    last = v.tensor_tensor(t2[:, :, ts], t2[:, :, ts], mid[:, :, n:n + 1].to_broadcast([P, C, P]),
                                           ALU.subtract)
                link(last)
                v.tensor_tensor(small[:, 20:23].unsqueeze(2), t2[:, :, P - 1:P], mid[:, :, 1:2], ALU.add)
                dve.wait_ge(S["kk_norm"], 1)
                link(v.reciprocal(t3, t3))
                link(v.tensor_tensor(t1, t1, t3, ALU.mult))
                tell(v.tensor_tensor(t3, t2, L1, ALU.subtract), "exp_in_ready")
                for c in range(C):
                    last = v.tensor_scalar(L3[:, c, :], L2[:, c, :], col("ka", c), small[:, 14 + c:15 + c],
                                           ALU.mult, ALU.add)
                link(last)
                link(v.tensor_tensor(sh[:, K_:K_ + 3, :], sh[:, K_:K_ + 3, :], L3, ALU.mult))
                link(v.tensor_tensor(L6, sh[:, R_:R_ + 3, :], sh[:, K_:K_ + 3, :], ALU.mult))
                for c in range(C):
                    last = v.tensor_scalar(L6[:, c, :], L6[:, c, :], col("rk", c), None, ALU.mult)
                tell(last, "bonus_in")
                dve.wait_ge(S["exps_ready"], 1)
                v.scalar_tensor_tensor(L3, t1, -1.0, t3, ALU.mult, ALU.mult)
                v.tensor_tensor(L4, sh[:, R_:R_ + 3, :], t2, ALU.mult)
                link(v.tensor_tensor(t1, t1, L2, ALU.mult))
                dve.wait_ge(S["bonus_sum"], 1)
                v.tensor_tensor(L5, t1, L1, ALU.mult)
                tell(v.tensor_tensor(L6, sh[:, K_:K_ + 3, :], L1, ALU.mult), "keys_ready")
                for cs, ps in pairs(2, 3):
                    last = v.tensor_tensor(L2[:, cs, :], ps, sh[:, V_ + cs.start:V_ + cs.stop, :], ALU.mult)
                tell(last, "bonus_ready")

                dve.wait_ge(S["bonus_ready"], 1)
                for i in range(3):
                    dve.wait_ge(S["rot_full"], i + 1)
                    dve.wait_ge(S["p_copied"], N_IN)
                    q = pT[:, RQ + 2 * i:RQ + 2 * i + 2, 1:T + 1]
                    tmp = t1[:, 0:2, :]
                    cos, sin = (K(k).unsqueeze(1).to_broadcast([P, 2, T]) for k in ("cos", "sin"))
                    tell(v.tensor_tensor(tmp, bank[4 + i % 2][:, :].rearrange("p (c t) -> p c t", c=2), sin, ALU.mult),
                         "rot_used")
                    link(v.tensor_tensor(q, q, cos, ALU.mult))
                    dve.wait_ge(S["rot_used"], i + 1)
                    if i < 2:
                        link(v.tensor_tensor(q, q, tmp, ALU.add))
                    else:
                        tell(v.tensor_tensor(q, q, tmp, ALU.add), "rotated")
                link(v.tensor_tensor(qxi, pT[:, RQ:RQ + 3, P + 1:T + 1], K("xi").rearrange("p (c t) -> p c t", c=C),
                                     ALU.mult))
                for g in range(4):
                    dve.wait_ge(S["ret_scores"], g + 1)
                    tell(v.tensor_tensor(sysTT[:, 3 * g:3 * g + 3, :],
                                         bank[g][:, 0:384].rearrange("p (c t) -> p c t", c=C),
                                         K("ret")[:, 384 * (g % 2):384 * (g % 2) + 384].rearrange("p (c t) -> p c t", c=C),
                                         ALU.mult), "ret_masked")
                dve.wait_ge(S["kret_full"], 1)
                tell(v.tensor_tensor(kret.rearrange("p (h d) -> p h d", h=H),
                                     bank[6][:, 0:384].rearrange("p (h d) -> p h d", h=H),
                                     K("zeta").unsqueeze(2).to_broadcast([P, H, 64]), ALU.mult), "kret_scaled")
                dve.wait_ge(S["ret_state"], 1)
                for p in range(2):
                    rows = slice(64 * p, 64 * p + 64)
                    last = v.tensor_copy(Rbd[rows, :, 64 * p:64 * p + 64],
                                         bank[7][rows, 0:384].rearrange("p (c i) -> p c i", c=C)[:, :, 64 * p:64 * p + 64])
                tell(last, "ret_state_kept")
                dve.wait_ge(S["ret_sums"], 1)
                for cs, ps in pairs(2, 3):
                    last = v.tensor_scalar(sh[:, 3 + cs.start:3 + cs.stop, :], ps, 1.0 / 64, EPS, ALU.mult, ALU.add)
                tell(last, "ret_clamped")

                def masked(dst, g, b, mask):
                    return v.tensor_tensor(dst[:, 3 * g:3 * g + 3, :],
                                           bank[b][:, 0:384].rearrange("p (c t) -> p c t", c=C),
                                           mask.unsqueeze(1).to_broadcast([P, C, P]), ALU.mult)

                def added(dst, g, b):
                    d = dst[:, 3 * g:3 * g + 3, :]
                    return v.tensor_tensor(d, bank[b][:, 0:384].rearrange("p (c t) -> p c t", c=C), d, ALU.add)

                for g in range(4):
                    dve.wait_ge(S["mab_full"], g + 1)
                    tell(masked(sysM, g, g, K("strict")), "mab_kept")
                for g in range(4):
                    dve.wait_ge(S["mab_full"], 4 + g + 1)
                    tell(masked(sysT, g, 4 + g, K("below1")), "mab_kept")
                dve.wait_ge(S["mab_kept"], 8)
                for g in range(4):
                    gg = slice(3 * g, 3 * g + 3)
                    eye = K("ident").unsqueeze(1).to_broadcast([P, C, P])
                    v.tensor_tensor(sysT[:, gg, :], sysT[:, gg, :], eye, ALU.add)
                    link(v.tensor_tensor(sysTT[:, gg, :], sysM[:, gg, :],
                                         K("above1").unsqueeze(1).to_broadcast([P, C, P]), ALU.mult))
                    tell(v.tensor_tensor(sysTT[:, gg, :], sysTT[:, gg, :], eye, ALU.add), "t_kept")
                below = con[:, at["below2"][0]:at["below64"][1]]

                def level(lv, mask, last_level):
                    for g in range(4):
                        dve.wait_ge(S["z_full"], lv * 4 + g + 1)
                        tell(masked(sysZ, g, g, mask), "z_kept")
                    for g in range(4):
                        dve.wait_ge(S["t_full"], lv * 4 + g + 1)
                        one = added(sysTT, g, 4 + g % 2 * 2)
                        if not last_level:
                            one = added(sysT, g, 5 + g % 2 * 2)
                        tell(one, "t_kept")

                with dve.Fori(0, 5) as lv:
                    level(lv, below[:, bass.ds(lv * P, P)], False)
                level(5, K("below64"), True)
                for i, (dst, b, mask) in enumerate(((sysM, 0, "strict"), (sysT, 4, "incl"), (sysZ, 0, "incl"))):
                    for g in range(4):
                        dve.wait_ge(S["m_full"], 4 * i + g + 1)
                        tell(masked(dst, g, b + g, K(mask)), "m_kept")
                dve.wait_ge(S["s_full"], 1)
                for c in range(C):
                    for p in range(2):
                        rows = slice(64 * p, 64 * p + 64)
                        last = v.tensor_scalar(Sbd[rows, c, 64 * p:64 * p + 64],
                                               bank[6][rows, c * P + 64 * p:c * P + 64 * p + 64],
                                               small[rows, 20 + c:21 + c], None, ALU.mult)
                tell(last, "s_kept")
                dve.wait_ge(S["ret_rms"], 1)
                link(v.reciprocal(sh[:, 3:6, :], sh[:, 3:6, :]))
                dve.wait_ge(S["gate_tanh"], 1)
                v.tensor_tensor(sh[:, 0:3, :], sh[:, 0:3, :], sh[:, 3:6, :], ALU.mult)
                link(v.scalar_tensor_tensor(sh[:, 6:9, :], sh[:, 6:9, :], 1.0, pT[:, RG:RG + 3, 1:T + 1],
                                            ALU.add, ALU.mult))
                v.scalar_tensor_tensor(hT[:, 3:6, :], sh[:, 0:3, :], 0.5, sh[:, 6:9, :], ALU.mult, ALU.mult)
                dve.wait_ge(S["pool_full"], 1)
                for c in range(2):
                    last = v.tensor_scalar(hT[:, 6 + c, :], bank[2][:, c * T:c * T + T], col("ps", c), None, ALU.mult)
                tell(last, "others_ready")
                dve.wait_ge(S["y_mean"], 1)
                for cs, ps in pairs(0, 1):
                    last = v.scalar_tensor_tensor(t2[:, cs, :], ps, -1.0 / 64, t2[:, cs, :], ALU.mult, ALU.add)
                link(last)
                tell(v.tensor_tensor(t1, t2, t2, ALU.mult), "y_centred")
                dve.wait_ge(S["y_var"], 1)
                for cs, ps in pairs(2, 3):
                    last = v.tensor_scalar(t3[:, cs, :], ps, 1.0 / 64, LNX_EPS, ALU.mult, ALU.add)
                tell(last, "y_clamped")
                dve.wait_ge(S["y_root"], 1)
                link(v.reciprocal(t3, t3))
                link(v.tensor_tensor(t2, t2, t3, ALU.mult))
                for c in range(C):
                    last = v.tensor_scalar(t2[:, c, :], t2[:, c, :], col("lw", c), col("lb", c), ALU.mult, ALU.add)
                link(last)
                link(v.tensor_tensor(t2, t2, L2, ALU.add))
                tell(v.tensor_tensor(hT[:, 0:3, :], t2, L7, ALU.mult), "mixed_ready")
                for i in range(N_OUT):
                    dve.wait_ge(mix_used, l * N_MIX + N_ADA + N_IN + i + 1)
                    for j in range(2):
                        c = 2 * i + j
                        last = v.scalar_tensor_tensor(xT[:, c, :], bank[4 + i][:, j * T:j * T + T],
                                                      modv[:, 16 + c:17 + c], xT[:, c, :], ALU.mult, ALU.add)
                tell(last, "x_updated")

                rms(2, 1)
                modulate(1, "h_ready")
                def lower_half(j, e, e2, h):
                    s = slot_of(e2, j)
                    cols = slice(1024 * h, 1024 * h + 1024)
                    dve.wait_ge(S["hi_ready"], e * 6 + (2 * j + h + 1))
                    tell(v.tensor_tensor(lower(s)[:, cols], slot(s)[:, cols], upper[:, s, cols].bitcast(F32),
                                         ALU.subtract), "w_ready")

                for j in range(2):
                    for h in range(2):
                        lower_half(j, 0, 0, h)
                dve.wait_ge(S["logit_tanh"], 1)
                link(v.tensor_scalar(score, score, 0.5, 0.5, ALU.mult, ALU.add))
                link(v.tensor_tensor(choice, score, rbias[:, :].unsqueeze(1).to_broadcast([P, NT, NEXP]), ALU.add))
                for n in range(NT):
                    for g in range(8):
                        last = v.max(gtop[:, n, g, :], choice[:, n, 8 * g:8 * g + 8])
                link(last)
                link(v.tensor_tensor(gsum.unsqueeze(3), gtop[:, :, :, 0:1], gtop[:, :, :, 1:2], ALU.add))
                for n in range(NT):
                    mine = gsum[:, n, :].unsqueeze(2).to_broadcast([P, 8, 8])
                    other = gsum[:, n, :].unsqueeze(1).to_broadcast([P, 8, 8])
                    v.tensor_tensor(cmpa, other, mine, ALU.is_gt)
                    link(v.tensor_tensor(cmpb, other, mine, ALU.is_equal))
                    link(v.tensor_tensor(cmpb, cmpb, K("before").rearrange("p (i j) -> p i j", i=8), ALU.mult))
                    link(v.tensor_tensor(cmpa, cmpa, cmpb, ALU.add))
                    link(v.tensor_reduce(gcnt[:, n, :], cmpa, AX.X, ALU.add))
                link(v.tensor_scalar(gcnt, gcnt, 3.5, -1e30, ALU.is_gt, ALU.mult))
                link(v.tensor_tensor(masked_.rearrange("p n (g k) -> p (n g) k", k=8),
                                     choice.rearrange("p n (g k) -> p (n g) k", k=8),
                                     gcnt.rearrange("p n g -> p (n g)").unsqueeze(2).to_broadcast([P, NT * 8, 8]),
                                     ALU.add))
                for n in range(NT):
                    last = v.max(top8[:, n, :], masked_[:, n, :])
                link(last)
                for n in range(NT):
                    last = v.match_replace(repl[:, n, :], top8[:, n, :], masked_[:, n, :], -3e38)
                link(last)
                link(v.tensor_scalar(sel, repl, -2e38, None, ALU.is_lt))
                link(v.tensor_tensor(wn, score, sel, ALU.mult))
                link(v.tensor_reduce(den[:, :, 0:1], wn, AX.X, ALU.add))
                link(v.reciprocal(den[:, :, 1:2], den[:, :, 0:1]))
                for n in range(NT):
                    last = v.tensor_scalar(wn[:, n, :], wn[:, n, :], den[:, n, 1:2], 2.5, ALU.mult, ALU.mult)
                tell(last, "sel_ready")
                dve.wait_ge(S["sel_ready"], 1)
                dve.wait_ge(S["shared_silu"], 1)
                dve.wait_ge(mix_used, l * N_MIX + N_MIX - 1)
                tell(v.tensor_tensor(shh.rearrange("p f t -> p (f t)"), shs.rearrange("p f t -> p (f t)"),
                                     bank[7][:, :], ALU.mult), "shared_hidden")
                for b in range(4):
                    dve.wait_ge(S["htok_copied"], b + 1)
                    cols = slice(b % 2 * 512, b % 2 * 512 + 512)
                    tell(v.tensor_tensor(htokL[:, b // 2, cols], bank[b][:, :], htokH[:, b // 2, cols].bitcast(F32),
                                         ALU.subtract), "htok_split")
                dve.wait_ge(S["rank_full"], 1)
                link(v.tensor_tensor(posn, bank[4][:, 0:NT * NEXP].rearrange("p (n e) -> p n e", n=NT), sel, ALU.mult))
                link(v.tensor_scalar(posn, posn, -1.0, None, ALU.add))
                def onehots(quad, b):
                    for n in range(NT):
                        place = posn[:, n, bass.ds(quad * 4, 4)]
                        last = v.tensor_tensor(G[:, b, n, :, :, :],
                                               K("iota")[:, 0:64].unsqueeze(1).unsqueeze(1).to_broadcast([P, 4, 2, 64]),
                                               place.unsqueeze(2).unsqueeze(3).to_broadcast([P, 4, 2, 64]), ALU.is_equal)
                    tell(last, "g_ready")

                onehots(0, 0)
                link(v.tensor_scalar(flags[0:64, :], K("blocks", 0, 64), bank[4][0:64, 128:129], None, ALU.is_lt))
                tell(v.tensor_reduce(fsum[0:64, :], flags[0:64, :], AX.X, ALU.add), "lists_in")
                link(v.tensor_copy(wHL[:, :, :, 0], wn))
                v.tensor_tensor(wHL[:, :, :, 1], wn, wHL[:, :, :, 0].bitcast(F32), ALU.subtract)
                dve.wait_ge(S["prefix_full"], 1)
                link(v.tensor_copy(fidx[0:64, 0:1], bank[5][0:64, 0:1]))
                for b in range(2):
                    link(v.tensor_tensor(fidx[0:64, b + 1:b + 2], fidx[0:64, b:b + 1], flags[0:64, b:b + 1], ALU.add))
                for b in range(3):
                    last = v.tensor_scalar(onehot[0:64, b, :], K("iota", 0, 64)[:, 0:32], fidx[0:64, b:b + 1],
                                           flags[0:64, b:b + 1], ALU.is_equal, ALU.mult)
                tell(last, "onehot_ready")
                dve.wait_ge(S["list_full"], 1)
                link(v.tensor_copy(oint[:, :], bank[5][0:1, 0:33]))
                v.tensor_scalar(oexp[:, :], oint[:, :], 2, None, ALU.logical_shift_right)
                tell(v.tensor_scalar(oblk[:, :], oint[:, :], 3, None, ALU.bitwise_and), "list_ready")
                dve.wait_ge(S["list_ready"], 1)
                def step(quad, u, b, last, onehots_too):
                    e = quad * 4 + u
                    if not (last and u == 3):
                        lower_half(0, e + 1, (u + 1) % 2, 1)
                    dve.wait_ge(S["silu_ready"], e + 1)
                    tell(v.tensor_tensor(hid, sg, bank[5][:, 128:256].rearrange("p (f s) -> p f s", f=2), ALU.mult),
                         "hid_ready")
                    dve.wait_ge(S["gt_full"], e + 1)
                    tell(v.tensor_reduce(wslot[:, 0:1], bank[7][:, 0:2], AX.X, ALU.add), "wslot_ready")
                    dve.wait_ge(S["hs_hi"], e + 1)
                    tell(v.tensor_tensor(hs[:, :, 1, :], hid, hs[:, :, 0, :].bitcast(F32), ALU.subtract), "hs_lo")
                    if not (last and u == 3):
                        lower_half(1, e + 1, (u + 1) % 2, 0)
                        lower_half(1, e + 1, (u + 1) % 2, 1)
                    for half in range(2):
                        cols = slice(512 * half, 512 * half + 512)
                        dve.wait_ge(S["y_hi"], e * 2 + (half + 1))
                        tell(v.scalar_tensor_tensor(yL[:, cols], bank[6 + half][:, :], wslot[:, 0:1],
                                                    yH[:, cols].bitcast(F32), ALU.mult, ALU.subtract), "y_lo")
                    if u == 3 and onehots_too:
                        onehots(quad + 2, b)
                    if not (last and u == 3):
                        lower_half(2, e + 1, (u + 1) % 2, 0)
                        lower_half(2, e + 1, (u + 1) % 2, 1)
                        if not (last and u == 2):
                            lower_half(0, e + 2, u % 2, 0)

                onehots(1, 1)
                for j, e, n in ((2, 0, 2), (0, 1, 1)):
                    for h in range(n):
                        lower_half(j, e, e, h)
                with dve.Fori(0, NEXP // 8 - 1) as it:
                    for b in range(2):
                        for u in range(4):
                            step(it * 2 + b, u, b, False, True)
                for b in range(2):
                    for u in range(4):
                        step(NEXP // 4 - 2 + b, u, b, b == 1, False)

                more = dve.value_load(oint[0:1, 32:33], min_val=0, max_val=31)
                with dve.If(more > 0):
                    with dve.Fori(0, more) as t:
                        e = dve.value_load(oexp[0:1, bass.ds(t, 1)], min_val=0, max_val=NEXP - 1)
                        b = dve.value_load(oblk[0:1, bass.ds(t, 1)], min_val=1, max_val=3)
                        numbers = K("iota")[:, bass.ds(b * 64, 64)]
                        for n in range(NT):
                            place = posn[:, n, bass.ds(e, 1)]
                            v.tensor_scalar(G[:, 0, n, 0, 0, :], numbers, place, None, ALU.is_equal)
                            last = v.tensor_scalar(oGw[:, n, :], numbers, place, wn[:, n, bass.ds(e, 1)],
                                                   ALU.is_equal, ALU.mult)
                        tell(last, "o_g_ready")
                        dve.wait_ge(S["o_silu_ready"], t * 2 + 2)
                        tell(v.tensor_tensor(hid, sg,
                                             bank[7][:, 128:256].rearrange("p (f s) -> p f s", f=2), ALU.mult),
                             "o_hidden_ready")
                    dve.wait_ge(S["o_scattered"], more)
                    dve.sem_inc(S["sync_steps"], 1)
                with dve.Else():
                    dve.nop()
                dve.wait_ge(S["scattered"], NEXP)
                for c in range(DC):
                    last = v.scalar_tensor_tensor(xT[:, c, :], bank[c // 2][:, c % 2 * T:c % 2 * T + T],
                                                  modv[:, 40 + c:41 + c], xT[:, c, :], ALU.mult, ALU.add)
                link(last)
                layer_end(dve, l)

            chain[0] = 0
            dve.wait_ge(S["fin_sums"], 1)
            tell(v.tensor_scalar(rstd[:, :], bank[4][:, 0:T], 1.0 / D, EPS, ALU.mult, ALU.add), "fin_mean")
            dve.wait_ge(S["fin_rms"], 1)
            link(v.reciprocal(rstd[:, :], rstd[:, :]))
            for c in range(DC):
                last = v.scalar_tensor_tensor(hT[:, c, :], xT[:, c, :], col("fg", c), rstd[:, :], ALU.mult, ALU.mult)
            tell(last, "fin_scaled")

        @block.tensor
        def _(pe):
            def mm(out_, lhsT, rhs, start=True, stop=True, **kw):
                return nc.tensor.matmul(out_, lhsT, rhs, start=start, stop=stop, **kw)

            def turn(out_, in_, n=P):
                return nc.tensor.transpose(out_, in_, K("ident", 0, n)[:, 0:n])

            def sumsq(b, told):
                for k in range(DC):
                    last = mm(bank[b][:, 0:T], K("ones"), hT[:, k, :], k == 0, k == DC - 1)
                last.then_inc(S[told], 1)

            def block_sums(src, b0, b1, told):
                for c in range(C):
                    last = mm(bank[(b0, b0, b1)[c]][:, c % 2 * T:c % 2 * T + T], K("block"), src[:, c, :])
                last.then_inc(S[told], 1)

            pe.wait_ge(S["consts"], 16)
            pe.wait_ge(S["silu_c"], 16)
            turn(bank[7][:, 0:DC], modr[0:DC, 0:P], DC).then_inc(S["silu_c"], 1)
            pe.wait_ge(S["x_loaded"], 16)
            for k in range(DC):
                if k == DC - 1:
                    pe.wait_ge(S["silu_c"], 18)
                for n in range(NT):
                    last = turn(bank[k][:, n * P:n * P + P], xtok[:, n, k * P:k * P + P])
                last.then_inc(S["x_turned"], 1)
            pe.wait_ge(S["x_moved"], DC)
            pe.wait_ge(S["silu_c"], 20)
            with pe.Fori(0, L) as l:
                for i in range(N_ADA):
                    if i == 14:
                        pe.wait_ge(S["params_loaded"], l * (16 * N_PARAM) + 16 * N_PARAM)
                        turn(bank[0][:, 0:NROW], prow[0:NROW, :], NROW).then_inc(S["params_moved"], 1)
                        pe.wait_ge(S["squares_ready"], 1)
                        sumsq(2, "sumsq_ready")
                    g, first = i // ADA_GROUP, i % ADA_GROUP == 0
                    if not first:
                        w = mix_wait(pe, l, i).rearrange("p (k n) -> p k n", k=DC)
                        for k in range(DC):
                            last = mm(bank[1][0:N_ADA, 0:2 * P], crow[:, k, N_ADA - 1 - i:2 * N_ADA - 1 - i], w[:, k, :],
                                      i == 1 and k == 0, True, skip_group_check=True)
                    if i % ADA_GROUP == 1:
                        pe.wait_ge(S["ada_summed"], g + 1)
                        j = i - 1
                        mm(bank[1][0:N_ADA, 0:2 * P], K("pick")[:, N_ADA - 1 - j:2 * N_ADA - 1 - j], adasum[:, g, :],
                           False, True, skip_group_check=True).then_inc(mix_used, 2)
                    elif not first:
                        last.then_inc(mix_used, 1)
                pe.wait_ge(S["mod_ready"], 1)
                for j in range(2):
                    last = turn(bank[3][:, N_ADA * j:N_ADA * j + N_ADA], modr[:, j * P:j * P + P], N_ADA)
                last.then_inc(S["mod_turned"], 1)
                pe.wait_ge(S["h_ready"], 1)
                for i in range(N_IN):
                    n = min(2, PC - 2 * i)
                    w = mix_wait(pe, l, N_ADA + i)[:, 0:DC * n * P].rearrange("p (k n) -> p k n", k=DC)
                    if i >= 2:
                        pe.wait_ge(S["p_copied"], i - 1)
                    for j in range(n):
                        for k in range(DC):
                            last = mm(bank[6 + i % 2][:, j * T:j * T + T], w[:, k, j * P:j * P + P], hT[:, k, :],
                                      k == 0, k == DC - 1)
                    last.then_inc(mix_used, 1)
                    if i == 7:
                        pe.wait_ge(S["tanh_w_ready"], 1)
                        for c in range(C):
                            last = mm(bank[c // 2][:, c % 2 * T:c % 2 * T + T], lora[0:64, c * P:c * P + P],
                                      lorin[0:64, :])
                        last.then_inc(S["lora_full"], 1)
                        for c in range(C):
                            last = mm(bank[2 + c // 2][:, c % 2 * T:c % 2 * T + T], lora[64:128, c * P:c * P + P],
                                      sh[64:128, LW, :])
                        last.then_inc(S["lora_full"], 1)
                        pe.wait_ge(S["kk_squares"], 1)
                        block_sums(t2, 4, 5, "kk_sums")
                    elif i == 9:
                        pe.wait_ge(S["sigx_ready"], 1)
                        pe.wait_ge(S["kk_clamped"], 1)
                        for c in range(C):
                            last = mm(bank[4 + c // 2][:, c % 2 * T:c % 2 * T + T], gup[:, c * P:c * P + P], sigx)
                        last.then_inc(S["lora_full"], 1)
                        pe.wait_ge(S["z_tanh"], 1)
                        for n in range(NT):
                            for c in range(C):
                                last = turn(bank[n][:, c * P:c * P + P], sh[:, V_ + c, n * P:n * P + P])
                            last.then_inc(S["vtok_full"], 1)
                    elif i == 10:
                        pe.wait_ge(S["bonus_in"], 1)
                        pe.wait_ge(S["a_tanh"], 1)
                        block_sums(L6, 2, 3, "bonus_sum")
                    elif i == 11:
                        pe.wait_ge(S["keys_ready"], 1)
                        for n, src in enumerate((L5, L6)):
                            pe.wait_ge(S["vtok_copied"], n + 1)
                            for c in range(C):
                                last = turn(bank[n][:, c * P:c * P + P], src[:, c, 0:P])
                            last.then_inc(S["btok_full"], 1)
                pe.wait_ge(S["p_copied"], N_IN)
                pe.wait_ge(S["g_copied"], 1)
                for i in range(3):
                    if i == 2:
                        pe.wait_ge(S["rot_used"], 1)
                    for j in range(2):
                        last = mm(bank[4 + i % 2][:, j * T:j * T + T], K("rot"), pT[:, RQ + 2 * i + j, 1:T + 1])
                    last.then_inc(S["rot_full"], 1)
                pe.wait_ge(S["rotated"], 1)
                pe.wait_ge(S["bonus_ready"], 1)
                pe.wait_ge(S["btok_copied"], 2)

                def inner(lhs, rhs, l0, r0, g, b):
                    n, p = g // 2, g % 2
                    rows = slice(64 * p, 64 * p + 64)
                    for c in range(C):
                        last = mm(bank[b][:, c * P:c * P + P], lhs[rows, l0 + c, n * P:n * P + P],
                                  rhs[rows, r0 + c, n * P:n * P + P])
                    return last

                pTv = pT[:, :, 1:T + 1]
                for g in range(4):
                    inner(pTv, pTv, RK, RQ, g, g).then_inc(S["ret_scores"], 1)
                for n in range(NT):
                    for c in range(C):
                        last = turn(bank[4 + n][:, c * P:c * P + P], pTv[:, RV + c, n * P:n * P + P])
                    last.then_inc(S["vret_full"], 1)
                pe.wait_ge(S["bonus_ready"], 1)
                for c in range(C):
                    last = turn(bank[6][:, c * P:c * P + P], pTv[:, RK + c, 0:P])
                last.then_inc(S["kret_full"], 1)
                pe.wait_ge(S["kret_scaled"], 1)
                pe.wait_ge(S["vret_copied"], 2)
                for c in range(C):
                    last = mm(bank[7][:, c * P:c * P + P], kret[:, c * P:c * P + P], vret[:, 0, c * P:c * P + P])
                last.then_inc(S["ret_state"], 1)
                pe.wait_ge(S["ret_masked"], 4)

                def outputs(b, n, terms, state, query):
                    for c in range(C):
                        if n:
                            mm(bank[b][:, c * P:c * P + P], state[:, c, :], query(c), True, False,
                               skip_group_check=True)
                        for p in range(2):
                            rows = slice(64 * p, 64 * p + 64)
                            h = 2 * c + p
                            for i, (vals, sys) in enumerate(terms):
                                last = mm(bank[b][rows, c * P:c * P + P], vals[:, n, 64 * h:64 * h + 64],
                                          sys[:, 3 * (2 * n + p) + c, :], n == 0 and i == 0, i == len(terms) - 1,
                                          skip_group_check=True)
                    return last

                for n in range(NT):
                    if n:
                        pe.wait_ge(S["ret_state_kept"], 1)
                    outputs(n, n, ((vret, sysTT),), Rbd, lambda c: qxi[:, c, :]).then_inc(S["ret_y_full"], 1)
                pe.wait_ge(S["ret_squares"], 1)
                block_sums(sh[:, 3:6, :], 2, 3, "ret_sums")

                pe.wait_ge(S["ret_y_copied"], 2)
                for g in range(4):
                    if g == 2:
                        pe.wait_ge(S["ret_clamped"], 1)
                    inner(L5, L3, 0, 0, g, g).then_inc(S["mab_full"], 1)
                for g in range(4):
                    inner(L3, L5, 0, 0, g, 4 + g).then_inc(S["mab_full"], 1)
                def level(lv, last_level):
                    for g in range(4):
                        pe.wait_ge(S["t_kept"], lv * 4 + (g + 1))
                        for c in range(C):
                            q = 3 * g + c
                            last = mm(bank[g][:, c * P:c * P + P], sysM[:, q, :], sysT[:, q, :])
                        last.then_inc(S["z_full"], 1)
                    for g in range(4):
                        pe.wait_ge(S["z_kept"], lv * 4 + (g + 1))
                        pe.wait_ge(S["t_kept"], lv * 4 + (g + 3))
                        for c in range(C):
                            q = 3 * g + c
                            last = mm(bank[4 + g % 2 * 2][:, c * P:c * P + P], sysZ[:, q, :], sysTT[:, q, :])
                        if not last_level:
                            for c in range(C):
                                q = 3 * g + c
                                last = mm(bank[5 + g % 2 * 2][:, c * P:c * P + P], sysTT[:, q, :], sysZ[:, q, :])
                        last.then_inc(S["t_full"], 1)

                with pe.Fori(0, 5) as lv:
                    level(lv, False)
                level(5, True)
                for i, (lhs, rhs, b) in enumerate(((L6, L3, 0), (L5, L4, 4), (L6, L4, 0))):
                    if i == 1:
                        pe.wait_ge(S["t_kept"], 28)
                    for g in range(4):
                        if i == 2:
                            pe.wait_ge(S["m_kept"], g + 1)
                        inner(lhs, rhs, 0, 0, g, b + g).then_inc(S["m_full"], 1)
                pe.wait_ge(S["m_kept"], 12)
                for n in range(NT):
                    b = (4, 7)[n]
                    if n:
                        pe.wait_ge(S["s_kept"], 1)
                    for c in range(C):
                        if n:
                            mm(bank[b][:, c * P:c * P + P], L3[:, c, P:T], Sbd[:, c, :], True, False,
                               skip_group_check=True)
                        for p in range(2):
                            h = 2 * c + p
                            last = mm(bank[b][:, 64 * h:64 * h + 64], sysM[:, 3 * (2 * n + p) + c, :],
                                      vtok[:, n, 64 * h:64 * h + 64], n == 0, True, skip_group_check=True)
                    last.then_inc(S["x_full"], 1)
                    pe.wait_ge(S["x_copied"], n + 1)
                    for h in range(H):
                        last = mm(bank[(5, 4)[n]][:, 64 * h:64 * h + 64], sysTT[:, 3 * (2 * n + h % 2) + h // 2, :],
                                  xsb[:, 64 * h:64 * h + 64])
                    last.then_inc(S["u_full"], 1)
                    pe.wait_ge(S["u_copied"], n + 1)
                    if n == 0:
                        for c in range(C):
                            cols = slice(c * P, c * P + P)
                            mm(bank[6][:, cols], btok[:, cols], utok[:, 0, cols], True, False)
                            last = mm(bank[6][:, cols], ktok[:, cols], vtok[:, 0, cols], False, True)
                        last.then_inc(S["s_full"], 1)
                    outputs(n, n, ((utok, sysT), (vtok, sysZ)), Sbd, lambda c: L4[:, c, P:T]).then_inc(S["y_full"], 1)
                pe.wait_ge(S["pool_in"], 1)
                for c in range(2):
                    last = mm(bank[2][:, c * T:c * T + T], poolw[:, c, :], pooled[:, c, :])
                last.then_inc(S["pool_full"], 1)
                pe.wait_ge(S["y_copied"], 2)
                block_sums(t2, 0, 1, "y_mean")

                def project(i, chunks):
                    w = mix_wait(pe, l, N_ADA + N_IN + i).rearrange("p (k n) -> p k n", k=DC)
                    for j in range(2):
                        for k in chunks:
                            last = mm(bank[4 + i][:, j * T:j * T + T], w[:, k, j * P:j * P + P], hT[:, k, :],
                                      j == 0 and k == C, True, skip_group_check=True)
                    return last

                pe.wait_ge(S["others_ready"], 1)
                project(0, range(C, DC))
                pe.wait_ge(S["y_centred"], 1)
                block_sums(t1, 2, 3, "y_var")
                for i in range(1, N_OUT):
                    project(i, range(C, DC))
                pe.wait_ge(S["mixed_ready"], 1)
                for i in range(N_OUT):
                    project(i, range(C)).then_inc(mix_used, 1)

                pe.wait_ge(S["squares_ready"], 2)
                sumsq(4, "sumsq_ready")
                pe.wait_ge(S["h_ready"], 2)
                for n in range(NT):
                    for k in range(DC):
                        last = mm(bank[5][:, n * NEXP:n * NEXP + NEXP], hT[:, k, n * P:n * P + P], wrt[:, k, :],
                                  k == 0, k == DC - 1)
                last.then_inc(S["logits_full"], 1)
                for b in range(4):
                    for i in range(4):
                        k, n = b % 2 * 4 + i, b // 2
                        last = turn(bank[b][:, i * P:i * P + P], hT[:, k, n * P:n * P + P])
                    last.then_inc(S["htok_full"], 1)
                for i in range(2):
                    w = mix_wait(pe, l, N_MIX - 3 + i).rearrange("p (k n) -> p k n", k=DC)
                    for f in range(2):
                        for k in range(DC):
                            last = mm(bank[6 + i][:, f * T:f * T + T], w[:, k, f * P:f * P + P], hT[:, k, :],
                                      k == 0, k == DC - 1)
                    last.then_inc(mix_used, 1)
                pe.wait_ge(S["sel_ready"], 1)
                mm(bank[4][:, 0:NEXP], K("incl"), sel[:, 0, :])
                mm(bank[4][:, NEXP:2 * NEXP], K("ones"), sel[:, 0, :], True, False)
                mm(bank[4][:, NEXP:2 * NEXP], K("incl"), sel[:, 1, :], False, True)
                mm(bank[4][0:64, 128:129], sel[:, 0, :], K("ones")[:, 0:1], True, False)
                mm(bank[4][0:64, 128:129], sel[:, 1, :], K("ones")[:, 0:1], False, True).then_inc(S["rank_full"], 1)

                def shared_down(chunks):
                    for c in chunks:
                        for f in range(2):
                            last = mm(bank[c // 2][:, c % 2 * T:c % 2 * T + T], w[:, f, c * P:c * P + P], shh[:, f, :],
                                      c % 2 == 0 and f == 0, True, skip_group_check=True)
                    return last

                pe.wait_ge(S["shared_hidden"], 1)
                pe.wait_ge(S["htok_split"], 4)
                w = mix_wait(pe, l, N_MIX - 1).rearrange("p (k n) -> p k n", k=2)
                shared_down(range(4))
                pe.wait_ge(S["lists_in"], 1)
                mm(bank[5][0:64, 0:1], K("strict", 0, 64)[:, 0:64], fsum[0:64, :]).then_inc(S["prefix_full"], 1)
                shared_down(range(4, DC)).then_inc(mix_used, 1)
                pe.wait_ge(S["onehot_ready"], 1)
                for b in range(3):
                    mm(bank[5][0:1, 0:32], K("ids", 0, 64)[:, b:b + 1], onehot[0:64, b, :], b == 0, b == 2)
                mm(bank[5][0:1, 32:33], fsum[0:64, :], K("ones", 0, 64)[:, 0:1]).then_inc(S["list_full"], 1)

                def gather(k, b, bk=4):
                    for h, src in enumerate((htokH, htokL)):
                        for n in range(NT):
                            last = mm(bank[bk][:, h * T:h * T + T], src[:, n, k * P:k * P + P], G[:, b, n, :, 0, :],
                                      n == 0, n == NT - 1)
                    last.then_inc(S["xg_full"], 1)

                def gate_up(e, e2, u, b):
                    for j in range(2):
                        pe.wait_ge(S["w_ready"], e * 6 + (2 * j + 2))
                        s = slot_of(e2, j)
                        for k in range(DC):
                            for h, src in enumerate((upper[:, s, :], lower(s))):
                                last = mm(bank[5][:, FH * j:FH * j + FH], xg[:, b, k, u, :, :].rearrange("p h s -> p (h s)"),
                                          src[:, FH * k:FH * k + FH], k == 0 and h == 0, k == DC - 1 and h == 1)
                    last.then_inc(gu_used, 1)

                def step(quad, u, b, last_quad):
                    e = quad * 4 + u
                    if not last_quad:
                        if u == 0:
                            pe.wait_ge(S["g_ready"], quad + 2)
                        pe.wait_ge(S["xg_copied"], e * 2 + 8)
                        gather(2 * u, 1 - b)
                    pe.wait_ge(S["gu_copied"], e + 1)
                    for f in range(4):
                        last = mm(bank[5][:, 64 * f:64 * f + 64], gu[:, P * f:P * f + P], K("twice"))
                    last.then_inc(S["sum_full"], 1)
                    for n in range(NT):
                        twice = G[:, b, n, u, :, :].rearrange("p h s -> p (h s)")
                        mm(bank[6][:, n * P:n * P + P], twice, identR)
                    for n in range(NT):
                        twice = G[:, b, n, u, :, :].rearrange("p h s -> p (h s)")
                        last = mm(bank[7][:, 0:2], twice, wHL[:, n, bass.ds(e, 1), :].rearrange("p e h -> p (e h)"),
                                  n == 0, n == NT - 1)
                    last.then_inc(S["gt_full"], 1)
                    if not last_quad:
                        pe.wait_ge(S["xg_copied"], e * 2 + 9)
                        gather(2 * u + 1, 1 - b)
                    pe.wait_ge(S["hs_lo"], e + 1)
                    pe.wait_ge(S["gt_copied"], e + 1)
                    pe.wait_ge(S["wslot_ready"], e + 1)
                    pe.wait_ge(S["w_ready"], e * 6 + 6)
                    s = slot_of(u % 2, 2)
                    for half in range(2):
                        for f in range(2):
                            for h, src in enumerate((upper[:, s, :], lower(s))):
                                last = mm(bank[6 + half][:, :], hs[:, f, :, :].rearrange("p h s -> p (h s)"),
                                          src[:, D * f + 512 * half:D * f + 512 * half + 512],
                                          f == 0 and h == 0, f == 1 and h == 1)
                        last.then_inc(d_used if half else S["y_lo_full"], 1)
                    if not (last_quad and u == 3):
                        if u == 3:
                            pe.wait_ge(S["xg_copied"], e * 2 + 10)
                        gate_up(e + 1, (u + 1) % 2, (u + 1) % 4, b if u < 3 else 1 - b)
                    pe.wait_ge(S["y_lo"], e * 2 + 2)
                    for c in range(DC):
                        for src in (yH, yL):
                            last = mm(bank[c // 2][:, c % 2 * T:c % 2 * T + T], src[:, c * P:c * P + P], GT, False, True,
                                      skip_group_check=True)
                    last.then_inc(S["scattered"], 1)

                pe.wait_ge(S["htok_copied"], 5)
                pe.wait_ge(S["g_ready"], 1)
                for k in range(DC):
                    if k >= 3:
                        pe.wait_ge(S["xg_copied"], k - 2)
                    gather(k, 0, FIRST_BANKS[k])
                pe.wait_ge(S["xg_copied"], DC)
                pe.wait_ge(S["list_ready"], 1)
                gate_up(0, 0, 0, 0)
                with pe.Fori(0, NEXP // 8 - 1) as it:
                    for b in range(2):
                        for u in range(4):
                            step(it * 2 + b, u, b, False)
                for b in range(2):
                    for u in range(4):
                        step(NEXP // 4 - 2 + b, u, b, b == 1)

                pe.wait_ge(S["list_ready"], 1)
                more = pe.value_load(oint[0:1, 32:33], min_val=0, max_val=31)
                pe.sem_inc(S["o_gu_full"], 1)
                pe.sem_inc(S["o_y_full"], 1)
                with pe.If(more > 0):
                    with pe.Fori(0, more) as t:
                        pe.wait_ge(S["o_g_ready"], t + 1)
                        for k in range(DC):
                            for n in range(NT):
                                for h, src in enumerate((htokH, htokL)):
                                    last = mm(bank[4][:, k * 64:k * 64 + 64], src[:, n, k * P:k * P + P],
                                              G[:, 0, n, 0, 0, :], n == 0 and h == 0, n == NT - 1 and h == 1)
                        last.then_inc(S["o_xg_full"], 1)
                        for n in range(NT):
                            last = nc.tensor.transpose(bank[5][0:64, n * P:n * P + P], oGw[:, n, :], K("ident"))
                        last.then_inc(S["o_xg_full"], 1)
                        pe.wait_ge(S["o_xg_copied"], t + 1)
                        pe.wait_ge(S["o_loaded"], t * 32 + 32)
                        for j in range(2):
                            w = slot(slot_of(0, j)).rearrange("p (k n) -> p k n", k=DC)
                            for k in range(DC):
                                last = mm(bank[6][0:64, FH * j:FH * j + FH], oxg[:, k, :], w[:, k, :],
                                          k == 0, k == DC - 1)
                        last.then_inc(S["o_gu_full"], 1)
                        pe.wait_ge(S["o_silu_ready"], t * 2 + 1)
                        for f in range(4):
                            last = mm(bank[7][:, 64 * f:64 * f + 64], gu[0:64, P * f:P * f + P],
                                      K("ident", 0, 64)[:, 0:64])
                        last.then_inc(S["o_gu_full"], 1)
                        pe.wait_ge(S["o_hidden_ready"], t + 1)
                        pe.wait_ge(S["o_gwt_copied"], t + 1)
                        pe.wait_ge(S["o_down_loaded"], t * 16 + 16)
                        w = slot(slot_of(0, 2)).rearrange("p (k n) -> p k n", k=2)
                        for half in range(2):
                            for f in range(2):
                                last = mm(bank[4 + half][0:64, :], hid[:, f, :], w[:, f, 512 * half:512 * half + 512],
                                          f == 0, f == 1)
                        last.then_inc(S["o_y_full"], 1)
                        pe.wait_ge(S["o_y_copied"], t + 1)
                        for c in range(DC):
                            last = mm(bank[c // 2][:, c % 2 * T:c % 2 * T + T], oy[0:64, c * P:c * P + P],
                                      oGwT[0:64, :], False, True, skip_group_check=True)
                        last.then_inc(S["o_scattered"], 1)
                with pe.Else():
                    pe.nop()
                layer_end(pe, l)

            pe.wait_ge(S["fin_squares"], 1)
            sumsq(4, "fin_sums")
            pe.wait_ge(S["fin_scaled"], 1)
            for b in range(4):
                for i in range(4):
                    k, n = b % 2 * 4 + i, b // 2
                    last = turn(bank[b][:, i * P:i * P + P], hT[:, k, n * P:n * P + P])
                last.then_inc(S["store_full"], 1)


_INS = ["x", "c", "norm1_g", "norm2_g", "w_ada", "b_ada", "w_in", "w_out", "rwkv_mu", "rwkv_w_up", "rwkv_w0",
        "rwkv_a_up", "rwkv_a0", "rwkv_g_up", "rwkv_k_k", "rwkv_k_a", "rwkv_r_k", "rwkv_lnx_w", "rwkv_lnx_b",
        "pool_w", "pool_scale", "w_router", "router_bias", "we_gate", "we_up", "we_down",
        "ws_gate", "ws_up", "ws_down", "final_g"]


def kernel(**inputs):
    import numpy as _np
    import concourse.bacc as _bacc
    from concourse import mybir as _mybir
    from concourse.bass_utils import run_bass_kernel_spmd as _run

    nc = _bacc.Bacc("TRN2", target_bir_lowering=False, num_devices=1)
    arrays, args = {}, []
    at, table = constants()
    for name in _INS + ["consts"]:
        a = table if name == "consts" else _np.ascontiguousarray(inputs[name])
        arrays[f"in_{name}"] = a
        args.append(nc.dram_tensor(f"in_{name}", a.shape, _mybir.dt.from_np(a.dtype), kind="ExternalInput").ap())
    args.append(nc.dram_tensor("out_0", (1, T, D), F32, kind="ExternalOutput").ap())
    hybrid_trunk(nc, at, *args)
    r = _run(nc, [arrays], core_ids=[0])
    return r.results[0]["out_0"]
```
